# Optimizing a Trainium2 kernel written in Bass

```python
import math
import jax, jax.numpy as jnp
from jax import lax
import numpy as np

D_MODEL = 1024
BATCH = 1
SEQ = 256
DEPTH = 2

GRID_W = 64
CTX_LEN = 256
EPS = 1e-6
ROPE_BASE = 10000.0
ATTN_BLOCK = 128

A_HEADS = 4
A_DK = 128
A_DV = 128
A_WIDTH = A_HEADS * A_DK
HGRN_CHUNK = 16
B_HEADS = 4
B_HALF = 64
B_DV = 2 * B_HALF
B_WIDTH = B_HEADS * B_DV
EVEN_IN = 5 * A_WIDTH + 3 * B_WIDTH
C_HEADS = 16
C_KV_HEADS = 4
C_HEAD_DIM = 64
C_WINDOW = 128
ODD_IN = (C_HEADS + 2 * C_KV_HEADS) * C_HEAD_DIM
N_EXPERTS = 16
N_GROUPS = 4
EXPERTS_PER_GROUP = N_EXPERTS // N_GROUPS
TOP_K = 2
D_EXPERT = 1024
MOE_BLOCK = 128

N_EVEN = (DEPTH + 1) // 2
N_ODD = DEPTH // 2


F32 = jnp.float32

def rms_norm(x, g):
    xf = x.astype(F32)
    y = xf * lax.rsqrt(jnp.mean(xf * xf, axis=-1, keepdims=True) + EPS)
    return (y * g.astype(F32)).astype(x.dtype)

def axial_rope_tables(n_tokens, dim):
    n_rows = n_tokens // GRID_W
    row = jnp.repeat(jnp.arange(n_rows), GRID_W).astype(F32)
    col = jnp.tile(jnp.arange(GRID_W), n_rows).astype(F32)
    half = dim // 2
    inv = 1.0 / (ROPE_BASE ** (jnp.arange(0, half, 2, dtype=F32) / half))
    ar = row[:, None] * inv
    ac = col[:, None] * inv
    ang = jnp.concatenate([ar, ar, ac, ac], axis=-1)
    return jnp.cos(ang), jnp.sin(ang)

def _rotate_half(x):
    x1, x2 = jnp.split(x, 2, axis=-1)
    return jnp.concatenate([-x2, x1], axis=-1)

def apply_axial_rope(x, cos, sin):
    xr, xc = jnp.split(x, 2, axis=-1)
    xrot = jnp.concatenate([_rotate_half(xr), _rotate_half(xc)], axis=-1)
    return (x * cos[None, :, None, :] + xrot * sin[None, :, None, :]).astype(x.dtype)

def hgrn2_scan(q, k, v, logf, s0):
    b_, t_, h_, _ = q.shape
    dv = v.shape[-1]
    n = t_ // HGRN_CHUNK

    def chunks(a):
        return a.astype(F32).reshape(b_, n, HGRN_CHUNK, h_, a.shape[-1])

    qc, kc, vc, lf = chunks(q), chunks(k), chunks(v), chunks(logf)
    cum = jnp.cumsum(lf, axis=2)
    total = cum[:, :, -1]
    tri = jnp.tril(jnp.ones((HGRN_CHUNK, HGRN_CHUNK), dtype=bool))
    diff = cum[:, :, :, None] - cum[:, :, None, :]
    decay = jnp.exp(jnp.where(tri[:, :, None, None], diff, -jnp.inf))
    scores = jnp.einsum('bnthk,bntshk,bnshk->bnhts', qc, decay, kc)
    o_intra = jnp.einsum('bnhts,bnshv->bnthv', scores, vc)
    q_in = qc * jnp.exp(cum)
    k_out = kc * jnp.exp(total[:, :, None] - cum)

    def step(state, inp):
        q_n, k_n, v_n, tot_n = inp
        o_n = jnp.einsum('bthk,bhkv->bthv', q_n, state)
        state = state * jnp.exp(tot_n)[..., None] + jnp.einsum('bshk,bshv->bhkv', k_n, v_n)
        return state, o_n

    xs = (jnp.moveaxis(q_in, 1, 0), jnp.moveaxis(k_out, 1, 0), jnp.moveaxis(vc, 1, 0), jnp.moveaxis(total, 1, 0))
    s_final, o_inter = lax.scan(step, s0, xs)
    o = o_intra + jnp.moveaxis(o_inter, 0, 1)
    return o.reshape(b_, t_, h_, dv), s_final

def hgrn2_mixer(p, pc, lb, onorm_g):
    b_ = p.shape[0]

    def heads(a):
        return a.reshape(a.shape[0], a.shape[1], A_HEADS, -1)

    def split(a):
        q, ff, fb, i, g = jnp.split(a, 5, axis=-1)
        q = heads(jax.nn.silu(q.astype(F32)) * (A_DK ** -0.5))
        return q, heads(ff), heads(fb), heads(i), heads(g)

    ql, ffl, fbl, il, gl = split(p)
    qc, ffc, fbc, ic, gc = split(pc)
    lb = lb.astype(F32).reshape(2, A_HEADS, A_DK)

    def gates(f_raw, lb_d):
        f = lb_d + (1.0 - lb_d) * jax.nn.sigmoid(f_raw.astype(F32))
        return 1.0 - f, jnp.log(f)

    def direction(d, reverse, f_lat, f_ctx):
        fl = (lambda a: jnp.flip(a, axis=1)) if reverse else (lambda a: a)
        k_c, lf_c = gates(f_ctx, lb[d])
        k_l, lf_l = gates(f_lat, lb[d])
        s0 = jnp.zeros((b_, A_HEADS, A_DK, A_DV), F32)
        o_c, s_c = hgrn2_scan(fl(qc), fl(k_c), fl(ic), fl(lf_c), s0)
        o_l, _ = hgrn2_scan(fl(ql), fl(k_l), fl(il), fl(lf_l), s_c)
        return fl(o_c), fl(o_l)

    oc_f, ol_f = direction(0, False, ffl, ffc)
    oc_b, ol_b = direction(1, True, fbl, fbc)

    def finish(o, g):
        y = rms_norm(o, onorm_g) * jax.nn.silu(g.astype(F32))
        return y.reshape(y.shape[0], y.shape[1], A_WIDTH)

    return finish(ol_f + ol_b, gl), finish(oc_f + oc_b, gc)

def diff_attention_mixer(p, pc, lam_p, subln_g, lambda_init, rope, need_ctx):
    b_, t_, _ = p.shape

    def split_qkv(a):
        bb, tt = a.shape[0], a.shape[1]
        q, k, v = jnp.split(a, 3, axis=-1)
        return (q.reshape(bb, tt, B_HEADS, 2, B_HALF), k.reshape(bb, tt, B_HEADS, 2, B_HALF),
                v.reshape(bb, tt, B_HEADS, B_DV))

    q, k, v = split_qkv(p)
    qc, kc, vc = split_qkv(pc)
    cos, sin = rope
    q = apply_axial_rope(q.reshape(b_, t_, 2 * B_HEADS, B_HALF), cos, sin).reshape(b_, t_, B_HEADS, 2, B_HALF)
    k = apply_axial_rope(k.reshape(b_, t_, 2 * B_HEADS, B_HALF), cos, sin).reshape(b_, t_, B_HEADS, 2, B_HALF)
    lam_p = lam_p.astype(F32)
    lam = jnp.exp(jnp.sum(lam_p[0] * lam_p[1])) - jnp.exp(jnp.sum(lam_p[2] * lam_p[3])) + lambda_init
    scale = B_HALF ** -0.5

    def attend(qb, keys, vals):
        s = jnp.einsum('bqhmd,bkhmd->bhmqk', qb, keys).astype(F32) * scale
        pm = jax.nn.softmax(s, axis=-1)
        a = pm[:, :, 0] - lam * pm[:, :, 1]
        return jnp.einsum('bhqk,bkhv->bqhv', a, vals)

    keys = jnp.concatenate([kc, k], axis=1)
    vals = jnp.concatenate([vc, v], axis=1)
    nb = t_ // ATTN_BLOCK
    qb = jnp.moveaxis(q.reshape(b_, nb, ATTN_BLOCK, B_HEADS, 2, B_HALF), 1, 0)
    o = lax.map(lambda blk: attend(blk, keys, vals), qb)
    o = jnp.moveaxis(o, 0, 1).reshape(b_, t_, B_HEADS, B_DV)

    def finish(o):
        y = rms_norm(o, subln_g) * (1.0 - lambda_init)
        return y.reshape(y.shape[0], y.shape[1], B_WIDTH)

    y = finish(o)
    yc = finish(attend(qc, kc, vc)) if need_ctx else None
    return y, yc

def even_layer_mixer(h, hc, w_in, w_out, lb, onorm_g, lam_p, subln_g, lambda_init, rope, need_ctx):
    p = h @ w_in
    pc = hc @ w_in
    ya, yac = hgrn2_mixer(p[..., :5 * A_WIDTH], pc[..., :5 * A_WIDTH], lb, onorm_g)
    yb, ybc = diff_attention_mixer(p[..., 5 * A_WIDTH:], pc[..., 5 * A_WIDTH:], lam_p, subln_g, lambda_init, rope, need_ctx)
    y = jnp.concatenate([ya, yb], axis=-1) @ w_out
    yc = (jnp.concatenate([yac, ybc], axis=-1) @ w_out) if need_ctx else None
    return y, yc

def _sink_attend(qb, parts, sink_logit):
    scale = C_HEAD_DIM ** -0.5
    logits = []
    for kk, _, valid in parts:
        s = jnp.einsum('bqkgd,bskd->bkgqs', qb, kk).astype(F32) * scale
        if valid is not None:
            s = jnp.where(valid, s, -jnp.inf)
        logits.append(s)
    b_, nq = qb.shape[0], qb.shape[1]
    sink_col = jnp.broadcast_to(sink_logit[None, :, :, None, None], (b_, C_KV_HEADS, C_HEADS // C_KV_HEADS, nq, 1))
    pr = jax.nn.softmax(jnp.concatenate([sink_col] + logits, axis=-1), axis=-1)
    out = 0.0
    off = 1
    for (_, vv, _), s in zip(parts, logits):
        n = s.shape[-1]
        out = out + jnp.einsum('bkgqs,bskd->bqkgd', pr[..., off:off + n], vv)
        off += n
    return out

def odd_layer_mixer(h, hc, w_qkv, w_out, sink, rope, need_ctx):
    b_, t_, d_ = h.shape
    n_ctx = hc.shape[1]
    grp = C_HEADS // C_KV_HEADS
    q_cols = C_HEADS * C_HEAD_DIM
    p = h @ w_qkv
    q = p[..., :q_cols].reshape(b_, t_, C_HEADS, C_HEAD_DIM)
    k, v = jnp.split(p[..., q_cols:], 2, axis=-1)
    k = k.reshape(b_, t_, C_KV_HEADS, C_HEAD_DIM)
    v = v.reshape(b_, t_, C_KV_HEADS, C_HEAD_DIM)
    if need_ctx:
        pc = hc @ w_qkv
        qc = pc[..., :q_cols].reshape(b_, n_ctx, C_KV_HEADS, grp, C_HEAD_DIM)
        kvc = pc[..., q_cols:]
    else:
        kvc = hc @ w_qkv[:, q_cols:]
    kc, vc = jnp.split(kvc, 2, axis=-1)
    kc = kc.reshape(b_, n_ctx, C_KV_HEADS, C_HEAD_DIM)
    vc = vc.reshape(b_, n_ctx, C_KV_HEADS, C_HEAD_DIM)
    cos, sin = rope
    q = apply_axial_rope(q, cos, sin).reshape(b_, t_, C_KV_HEADS, grp, C_HEAD_DIM)
    k = apply_axial_rope(k, cos, sin)
    sink_logit = sink.astype(F32).reshape(C_KV_HEADS, grp)
    pad = ((0, 0), (C_WINDOW, C_WINDOW), (0, 0), (0, 0))
    kp = jnp.pad(k, pad)
    vp = jnp.pad(v, pad)
    span = ATTN_BLOCK + 2 * C_WINDOW
    nb = t_ // ATTN_BLOCK

    def block(n):
        start = n * ATTN_BLOCK
        qb = lax.dynamic_slice_in_dim(q, start, ATTN_BLOCK, axis=1)
        kb = lax.dynamic_slice_in_dim(kp, start, span, axis=1)
        vb = lax.dynamic_slice_in_dim(vp, start, span, axis=1)
        qpos = start + jnp.arange(ATTN_BLOCK)
        kpos = start - C_WINDOW + jnp.arange(span)
        valid = (jnp.abs(qpos[:, None] - kpos[None, :]) <= C_WINDOW) & (kpos[None, :] >= 0) & (kpos[None, :] < t_)
        return _sink_attend(qb, [(kc, vc, None), (kb, vb, valid)], sink_logit)

    o = lax.map(block, jnp.arange(nb))
    y = jnp.moveaxis(o, 0, 1).reshape(b_, t_, d_) @ w_out
    yc = None
    if need_ctx:
        yc = _sink_attend(qc, [(kc, vc, None)], sink_logit).reshape(b_, n_ctx, d_) @ w_out
    return y, yc

def routed_moe(h2d, router_w, router_b, w_gate, w_up, w_down):
    n_tok, d_ = h2d.shape
    aff = jax.nn.sigmoid(jnp.dot(h2d, router_w).astype(F32))
    sel = (aff + router_b.astype(F32)).reshape(n_tok, N_GROUPS, EXPERTS_PER_GROUP)
    group_score = jnp.sum(lax.top_k(sel, TOP_K)[0], axis=-1)
    grp = jnp.argmax(group_score, axis=-1)
    in_group = jnp.take_along_axis(sel, grp[:, None, None], axis=1)[:, 0]
    _, local = lax.top_k(in_group, TOP_K)
    expert = (grp[:, None] * EXPERTS_PER_GROUP + local).astype(jnp.int32)
    wts = jnp.take_along_axis(aff, expert, axis=1)
    wts = wts / jnp.sum(wts, axis=-1, keepdims=True)
    n_assign = n_tok * TOP_K
    n_blocks = -(-n_assign // MOE_BLOCK) + N_EXPERTS
    n_rows = n_blocks * MOE_BLOCK
    flat_e = expert.reshape(-1)
    flat_t = jnp.repeat(jnp.arange(n_tok, dtype=jnp.int32), TOP_K)
    flat_w = wts.reshape(-1)
    order = jnp.argsort(flat_e)
    e_sorted = flat_e[order]
    counts = jnp.bincount(flat_e, length=N_EXPERTS)
    padded = (counts + MOE_BLOCK - 1) // MOE_BLOCK * MOE_BLOCK
    pad_end = jnp.cumsum(padded)
    pad_start = pad_end - padded
    start = jnp.cumsum(counts) - counts
    dest = pad_start[e_sorted] + jnp.arange(n_assign) - start[e_sorted]
    row_tok = jnp.full((n_rows,), n_tok, jnp.int32).at[dest].set(flat_t[order])
    row_w = jnp.zeros((n_rows,), F32).at[dest].set(flat_w[order])
    block_start = jnp.arange(n_blocks) * MOE_BLOCK
    block_e = jnp.minimum(jnp.sum(pad_end[None, :] <= block_start[:, None], axis=1), N_EXPERTS - 1)
    x_pad = jnp.concatenate([h2d, jnp.zeros((1, d_), h2d.dtype)], axis=0)
    xb = x_pad[row_tok].reshape(n_blocks, MOE_BLOCK, d_)

    def expert_block(args):
        xblk, e = args
        hid = jax.nn.silu(xblk @ w_gate[e]) * (xblk @ w_up[e])
        return hid @ w_down[e]

    yb = lax.map(expert_block, (xb, block_e)).reshape(n_rows, d_)
    out = jnp.zeros((n_tok + 1, d_), F32).at[row_tok].add(yb * row_w[:, None])
    return out[:n_tok]

def first_inputs(seed: int = 0) -> dict:
    key = jax.random.key(seed)
    ks = jax.random.split(key, 24)
    d = D_MODEL
    nrm = jax.random.normal
    return {
        'x': nrm(ks[0], (BATCH, SEQ, d), F32),
        'c': nrm(ks[1], (BATCH, d), F32),
        'ctx': nrm(ks[2], (BATCH, CTX_LEN, d), F32),
        'c_ctx': nrm(ks[3], (d,), F32),
        'ada_w': nrm(ks[4], (DEPTH, d, 6 * d), F32) * (0.5 * d ** -0.5),
        'ada_b': nrm(ks[5], (DEPTH, 6 * d), F32) * 0.02,
        'norm_mix_g': 1.0 + 0.02 * nrm(ks[6], (DEPTH, d), F32),
        'norm_ffn_g': 1.0 + 0.02 * nrm(ks[7], (DEPTH, d), F32),
        'even_w_in': nrm(ks[8], (N_EVEN, d, EVEN_IN), F32) * d ** -0.5,
        'even_w_out': nrm(ks[9], (N_EVEN, A_WIDTH + B_WIDTH, d), F32) * (A_WIDTH + B_WIDTH) ** -0.5,
        'hgrn_lb_logits': 0.1 * nrm(ks[10], (DEPTH + 1, 2, A_WIDTH), F32),
        'hgrn_onorm_g': 1.0 + 0.02 * nrm(ks[11], (N_EVEN, A_DV), F32),
        'diff_lambda': 0.1 * nrm(ks[12], (N_EVEN, 4, B_HALF), F32),
        'diff_subln_g': 1.0 + 0.02 * nrm(ks[13], (N_EVEN, B_DV), F32),
        'odd_w_qkv': nrm(ks[14], (N_ODD, d, ODD_IN), F32) * d ** -0.5,
        'odd_w_out': nrm(ks[15], (N_ODD, C_HEADS * C_HEAD_DIM, d), F32) * (C_HEADS * C_HEAD_DIM) ** -0.5,
        'swa_sink': 0.5 * nrm(ks[16], (N_ODD, C_HEADS), F32),
        'router_w': nrm(ks[17], (d, N_EXPERTS), F32) * d ** -0.5,
        'router_b': 0.01 * nrm(ks[18], (N_EXPERTS,), F32),
        'moe_w_gate': nrm(ks[19], (DEPTH, N_EXPERTS, d, D_EXPERT), F32) * d ** -0.5,
        'moe_w_up': nrm(ks[20], (DEPTH, N_EXPERTS, d, D_EXPERT), F32) * d ** -0.5,
        'moe_w_down': nrm(ks[21], (DEPTH, N_EXPERTS, D_EXPERT, d), F32) * D_EXPERT ** -0.5,
        'final_norm_g': 1.0 + 0.02 * nrm(ks[22], (d,), F32),
    }

def first_block(x, c, ctx, c_ctx, ada_w, ada_b, norm_mix_g, norm_ffn_g, even_w_in, even_w_out,
              hgrn_lb_logits, hgrn_onorm_g, diff_lambda, diff_subln_g, odd_w_qkv, odd_w_out, swa_sink,
              router_w, router_b, moe_w_gate, moe_w_up, moe_w_down, final_norm_g):
    b_, t_, d_ = x.shape
    n_ctx = ctx.shape[1]
    rope_b = axial_rope_tables(t_, B_HALF)
    rope_c = axial_rope_tables(t_, C_HEAD_DIM)
    lower_bounds = jnp.cumsum(jax.nn.softmax(hgrn_lb_logits.astype(F32), axis=0), axis=0)
    xc = ctx
    for layer in range(DEPTH):
        last = layer == DEPTH - 1
        w_ada, b_ada = ada_w[layer], ada_b[layer]
        mod = (jax.nn.silu(c) @ w_ada + b_ada)[:, None, :]
        mod_c = (jax.nn.silu(c_ctx) @ w_ada + b_ada)[None, None, :]
        sh1, sc1, g1, sh2, sc2, g2 = jnp.split(mod, 6, axis=-1)
        csh1, csc1, cg1, csh2, csc2, cg2 = jnp.split(mod_c, 6, axis=-1)
        h = rms_norm(x, norm_mix_g[layer]) * (1.0 + sc1) + sh1
        hc = rms_norm(xc, norm_mix_g[layer]) * (1.0 + csc1) + csh1
        if layer % 2 == 0:
            j = layer // 2
            lambda_init = 0.8 - 0.6 * math.exp(-0.3 * layer)
            y, yc = even_layer_mixer(h, hc, even_w_in[j], even_w_out[j], lower_bounds[layer], hgrn_onorm_g[j],
                                     diff_lambda[j], diff_subln_g[j], lambda_init, rope_b, not last)
        else:
            j = layer // 2
            y, yc = odd_layer_mixer(h, hc, odd_w_qkv[j], odd_w_out[j], swa_sink[j], rope_c, not last)
        x = x + g1 * y
        h2 = rms_norm(x, norm_ffn_g[layer]) * (1.0 + sc2) + sh2
        if last:
            f = routed_moe(h2.reshape(-1, d_), router_w, router_b,
                           moe_w_gate[layer], moe_w_up[layer], moe_w_down[layer])
            x = x + g2 * f.reshape(b_, t_, d_)
        else:
            xc = xc + cg1 * yc
            hc2 = rms_norm(xc, norm_ffn_g[layer]) * (1.0 + csc2) + csh2
            tokens = jnp.concatenate([h2.reshape(-1, d_), hc2.reshape(-1, d_)], axis=0)
            f = routed_moe(tokens, router_w, router_b, moe_w_gate[layer], moe_w_up[layer], moe_w_down[layer])
            x = x + g2 * f[:b_ * t_].reshape(b_, t_, d_)
            xc = xc + cg2 * f[b_ * t_:].reshape(b_, n_ctx, d_)
    return rms_norm(x, final_norm_g)


DEPTH_2 = 1

D_MIX = D_MODEL
ATTN_HEADS = 4
QK_NOPE_DIM = 128
QK_ROPE_DIM = 64
QK_HEAD_DIM = QK_NOPE_DIM + QK_ROPE_DIM
V_HEAD_DIM = 128
ATTN_WIDTH = ATTN_HEADS * V_HEAD_DIM
Q_LORA_RANK = 256
KV_LORA_RANK = 128
ROPE_THETA = 10000.0
Q_BLOCK = 128
LRU_WIDTH = D_MIX - ATTN_WIDTH
LRU_HEADS = 4
LRU_BLOCK = LRU_WIDTH // LRU_HEADS
CONV_WIDTH = 4
LRU_C = 8.0
IN_SPLITS = [Q_LORA_RANK,
             Q_LORA_RANK + KV_LORA_RANK,
             Q_LORA_RANK + KV_LORA_RANK + QK_ROPE_DIM,
             Q_LORA_RANK + KV_LORA_RANK + QK_ROPE_DIM + LRU_WIDTH]
IN_PROJ_WIDTH = Q_LORA_RANK + KV_LORA_RANK + QK_ROPE_DIM + 2 * LRU_WIDTH
EXPERTS_PER_GROUP_2 = 8
N_EXPERTS_2 = N_GROUPS * EXPERTS_PER_GROUP_2
D_FF_EXPERT = 256


def rms_norm_2(x, g):
    xf = x.astype(jnp.float32)
    y = xf * lax.rsqrt(jnp.mean(xf * xf, axis=-1, keepdims=True) + EPS)
    return (y * g.astype(jnp.float32)).astype(x.dtype)

def rope_cos_sin(positions):
    inv = 1.0 / (ROPE_THETA ** (jnp.arange(0, QK_ROPE_DIM, 2, dtype=jnp.float32) / QK_ROPE_DIM))
    ang = positions.astype(jnp.float32)[..., None] * inv
    return jnp.cos(ang), jnp.sin(ang)

def apply_rope(x, cos, sin):
    xf = x.astype(jnp.float32)
    x1, x2 = jnp.split(xf, 2, axis=-1)
    c = cos[:, :, None, :]
    s = sin[:, :, None, :]
    return jnp.concatenate([x1 * c - x2 * s, x2 * c + x1 * s], axis=-1).astype(x.dtype)

def mla_attention(q_lat, kv_lat, k_rope, cos, sin, q_a_norm, w_q_b, kv_a_norm, w_kv_b, q_norm, k_norm):
    B, S, _ = q_lat.shape
    q = (rms_norm_2(q_lat, q_a_norm) @ w_q_b).reshape(B, S, ATTN_HEADS, QK_HEAD_DIM)
    kv = (rms_norm_2(kv_lat, kv_a_norm) @ w_kv_b).reshape(B, S, ATTN_HEADS, QK_NOPE_DIM + V_HEAD_DIM)
    k_nope, v = kv[..., :QK_NOPE_DIM], kv[..., QK_NOPE_DIM:]
    k_pe = jnp.broadcast_to(k_rope[:, :, None, :], (B, S, ATTN_HEADS, QK_ROPE_DIM))
    k = jnp.concatenate([k_nope, k_pe], axis=-1)
    q = rms_norm_2(q, q_norm)
    k = rms_norm_2(k, k_norm)
    q = jnp.concatenate([q[..., :QK_NOPE_DIM], apply_rope(q[..., QK_NOPE_DIM:], cos, sin)], axis=-1)
    k = jnp.concatenate([k[..., :QK_NOPE_DIM], apply_rope(k[..., QK_NOPE_DIM:], cos, sin)], axis=-1)
    qh = q.transpose(0, 2, 1, 3)
    kh = k.transpose(0, 2, 1, 3)
    vh = v.transpose(0, 2, 1, 3)
    n_blocks = S // Q_BLOCK
    q_blocks = qh.reshape(B, ATTN_HEADS, n_blocks, Q_BLOCK, QK_HEAD_DIM).transpose(2, 0, 1, 3, 4)
    key_idx = jnp.arange(S)
    scale = QK_HEAD_DIM ** -0.5

    def block(args):
        qb, bi = args
        s = jnp.einsum('bhqd,bhkd->bhqk', qb, kh, preferred_element_type=jnp.float32) * scale
        q_idx = bi * Q_BLOCK + jnp.arange(Q_BLOCK)
        s = jnp.where(key_idx[None, :] <= q_idx[:, None], s, -jnp.inf)
        p = jax.nn.softmax(s, axis=-1)
        return jnp.einsum('bhqk,bhkd->bhqd', p.astype(vh.dtype), vh)

    out = lax.map(block, (q_blocks, jnp.arange(n_blocks)))
    return out.transpose(1, 0, 3, 2, 4).reshape(B, S, ATTN_WIDTH)

def rg_lru_branch(x_lru, g_lru, positions, conv_w, conv_b, w_a, b_a, w_x, b_x, lam):
    B, S, C = x_lru.shape
    xc = lax.conv_general_dilated(x_lru, conv_w[:, None, :], window_strides=(1,),
                                  padding=[(CONV_WIDTH - 1, 0)],
                                  dimension_numbers=('NWC', 'WIO', 'NWC'),
                                  feature_group_count=C) + conv_b
    xb = xc.reshape(B, S, LRU_HEADS, LRU_BLOCK)
    r = jax.nn.sigmoid(jnp.einsum('bshi,hij->bshj', xb, w_a).reshape(B, S, C) + b_a)
    i = jax.nn.sigmoid(jnp.einsum('bshi,hij->bshj', xb, w_x).reshape(B, S, C) + b_x)
    log_a = -LRU_C * r.astype(jnp.float32) * jax.nn.softplus(-lam.astype(jnp.float32))
    a = jnp.exp(log_a)
    mult = jnp.sqrt(jnp.maximum(1.0 - jnp.exp(2.0 * log_a), 0.0))
    reset = (positions == 0)[..., None]
    a = jnp.where(reset, 0.0, a)
    mult = jnp.where(reset, 1.0, mult)
    b = mult * (i.astype(jnp.float32) * xc.astype(jnp.float32))

    def combine(lhs, rhs):
        a1, b1 = lhs
        a2, b2 = rhs
        return a1 * a2, a2 * b1 + b2

    _, h = lax.associative_scan(combine, (a, b), axis=1)
    return h.astype(x_lru.dtype) * jax.nn.gelu(g_lru)

def hierarchical_moe(h, w_rg, b_rg, w_re, b_re, w_gate, w_up, w_down):
    B, S, D = h.shape
    N = B * S
    t = h.reshape(N, D)
    g_prob = jax.nn.softmax((t @ w_rg).astype(jnp.float32) + b_rg, axis=-1)
    g_p, g_idx = lax.top_k(g_prob, 1)
    e_logits = ((t @ w_re).astype(jnp.float32) + b_re).reshape(N, N_GROUPS, EXPERTS_PER_GROUP_2)
    e_logits = jnp.take_along_axis(e_logits, g_idx[:, :, None], axis=1)[:, 0]
    e_p, e_idx = lax.top_k(jax.nn.softmax(e_logits, axis=-1), TOP_K)
    e_p = e_p / jnp.sum(e_p, axis=-1, keepdims=True)
    weights = g_p * e_p
    expert = g_idx * EXPERTS_PER_GROUP_2 + e_idx
    NK = N * TOP_K
    flat_e = expert.reshape(NK)
    flat_tok = jnp.repeat(jnp.arange(N, dtype=jnp.int32), TOP_K)
    flat_w = weights.reshape(NK)
    order = jnp.argsort(flat_e)
    sorted_e = flat_e[order]
    counts = jnp.bincount(flat_e, length=N_EXPERTS_2)
    padded = (counts + MOE_BLOCK - 1) // MOE_BLOCK * MOE_BLOCK
    starts = jnp.cumsum(counts) - counts
    pad_ends = jnp.cumsum(padded)
    pad_starts = pad_ends - padded
    dest = pad_starts[sorted_e] + (jnp.arange(NK) - starts[sorted_e])
    cap = (NK + N_EXPERTS_2 * (MOE_BLOCK - 1) + MOE_BLOCK - 1) // MOE_BLOCK * MOE_BLOCK
    n_blocks = cap // MOE_BLOCK
    row_tok = jnp.full((cap,), N, jnp.int32).at[dest].set(flat_tok[order])
    row_w = jnp.zeros((cap,), jnp.float32).at[dest].set(flat_w[order])
    block_e = jnp.minimum(jnp.searchsorted(pad_ends, jnp.arange(n_blocks) * MOE_BLOCK, side='right'),
                          N_EXPERTS_2 - 1)
    t_pad = jnp.concatenate([t, jnp.zeros((1, D), t.dtype)], axis=0)

    def expert_block(args):
        rows, e = args
        xb = t_pad[rows]
        hid = jax.nn.silu(xb @ w_gate[e]) * (xb @ w_up[e])
        return hid @ w_down[e]

    y_rows = lax.map(expert_block, (row_tok.reshape(n_blocks, MOE_BLOCK), block_e))
    y_rows = y_rows.reshape(cap, D).astype(jnp.float32) * row_w[:, None]
    y = jnp.zeros((N + 1, D), jnp.float32).at[row_tok].add(y_rows)[:N]
    return y.reshape(B, S, D).astype(h.dtype)

def hybrid_layer(x, c, positions, cos, sin, w_ada, b_ada, norm1_g, w_in, q_a_norm, w_q_b, kv_a_norm,
                 w_kv_b, q_norm, k_norm, conv_w, conv_b, lru_wa, lru_ba, lru_wx, lru_bx, lru_lambda,
                 attn_out_norm, lru_out_norm, w_out, norm2_g, w_router_group, b_router_group,
                 w_router_expert, b_router_expert, w_gate, w_up, w_down):
    mod = jax.nn.silu(c) @ w_ada + b_ada
    shift1, scale1, gate1, shift2, scale2, gate2 = jnp.split(mod[:, None, :], 6, axis=-1)
    h = rms_norm_2(x, norm1_g) * (1.0 + scale1) + shift1
    proj = h @ w_in
    q_lat, kv_lat, k_rope, x_lru, g_lru = jnp.split(proj, IN_SPLITS, axis=-1)
    attn = mla_attention(q_lat, kv_lat, k_rope, cos, sin, q_a_norm, w_q_b, kv_a_norm, w_kv_b,
                         q_norm, k_norm)
    lru = rg_lru_branch(x_lru, g_lru, positions, conv_w, conv_b, lru_wa, lru_ba, lru_wx, lru_bx,
                        lru_lambda)
    mixed = jnp.concatenate([rms_norm_2(attn, attn_out_norm), rms_norm_2(lru, lru_out_norm)], axis=-1)
    x = x + gate1 * (mixed @ w_out)
    h2 = rms_norm_2(x, norm2_g) * (1.0 + scale2) + shift2
    x = x + gate2 * hierarchical_moe(h2, w_router_group, b_router_group, w_router_expert,
                                     b_router_expert, w_gate, w_up, w_down)
    return x

def second_inputs(seed: int = 0) -> dict:
    key = jax.random.key(seed)
    ks = iter(jax.random.split(key, 40))
    L = DEPTH_2

    def normal(shape, scale):
        return jax.random.normal(next(ks), shape, jnp.float32) * scale

    def gain(n):
        return 1.0 + normal((L, n), 0.02)

    u = jax.random.uniform(next(ks), (L, LRU_WIDTH), jnp.float32, 0.9, 0.999)
    s = u ** (1.0 / LRU_C)
    lam = jnp.log(s) - jnp.log1p(-s)
    return {
        'x': normal((BATCH, SEQ, D_MODEL), 1.0),
        'c': normal((BATCH, D_MODEL), 1.0),
        'positions': jnp.tile(jnp.arange(SEQ, dtype=jnp.int32)[None, :], (BATCH, 1)),
        'w_ada': normal((L, D_MODEL, 6 * D_MODEL), D_MODEL ** -0.5),
        'b_ada': normal((L, 6 * D_MODEL), 0.02),
        'norm1_g': gain(D_MODEL),
        'w_in': normal((L, D_MODEL, IN_PROJ_WIDTH), D_MODEL ** -0.5),
        'q_a_norm': gain(Q_LORA_RANK),
        'w_q_b': normal((L, Q_LORA_RANK, ATTN_HEADS * QK_HEAD_DIM), Q_LORA_RANK ** -0.5),
        'kv_a_norm': gain(KV_LORA_RANK),
        'w_kv_b': normal((L, KV_LORA_RANK, ATTN_HEADS * (QK_NOPE_DIM + V_HEAD_DIM)), KV_LORA_RANK ** -0.5),
        'q_norm': gain(QK_HEAD_DIM),
        'k_norm': gain(QK_HEAD_DIM),
        'conv_w': normal((L, CONV_WIDTH, LRU_WIDTH), CONV_WIDTH ** -0.5),
        'conv_b': normal((L, LRU_WIDTH), 0.02),
        'lru_wa': normal((L, LRU_HEADS, LRU_BLOCK, LRU_BLOCK), LRU_BLOCK ** -0.5),
        'lru_ba': normal((L, LRU_WIDTH), 0.02),
        'lru_wx': normal((L, LRU_HEADS, LRU_BLOCK, LRU_BLOCK), LRU_BLOCK ** -0.5),
        'lru_bx': normal((L, LRU_WIDTH), 0.02),
        'lru_lambda': lam,
        'attn_out_norm': gain(ATTN_WIDTH),
        'lru_out_norm': gain(LRU_WIDTH),
        'w_out': normal((L, D_MIX, D_MODEL), D_MIX ** -0.5),
        'norm2_g': gain(D_MODEL),
        'w_router_group': normal((L, D_MODEL, N_GROUPS), D_MODEL ** -0.5),
        'b_router_group': normal((L, N_GROUPS), 0.01),
        'w_router_expert': normal((L, D_MODEL, N_EXPERTS_2), D_MODEL ** -0.5),
        'b_router_expert': normal((L, N_EXPERTS_2), 0.01),
        'w_gate': normal((L, N_EXPERTS_2, D_MODEL, D_FF_EXPERT), D_MODEL ** -0.5),
        'w_up': normal((L, N_EXPERTS_2, D_MODEL, D_FF_EXPERT), D_MODEL ** -0.5),
        'w_down': normal((L, N_EXPERTS_2, D_FF_EXPERT, D_MODEL), D_FF_EXPERT ** -0.5),
    }

def second_block(x, c, positions, w_ada, b_ada, norm1_g, w_in, q_a_norm, w_q_b, kv_a_norm, w_kv_b,
              q_norm, k_norm, conv_w, conv_b, lru_wa, lru_ba, lru_wx, lru_bx, lru_lambda,
              attn_out_norm, lru_out_norm, w_out, norm2_g, w_router_group, b_router_group,
              w_router_expert, b_router_expert, w_gate, w_up, w_down):
    cos, sin = rope_cos_sin(positions)
    for l in range(DEPTH_2):
        x = hybrid_layer(x, c, positions, cos, sin, w_ada[l], b_ada[l], norm1_g[l], w_in[l],
                         q_a_norm[l], w_q_b[l], kv_a_norm[l], w_kv_b[l], q_norm[l], k_norm[l],
                         conv_w[l], conv_b[l], lru_wa[l], lru_ba[l], lru_wx[l], lru_bx[l],
                         lru_lambda[l], attn_out_norm[l], lru_out_norm[l], w_out[l], norm2_g[l],
                         w_router_group[l], b_router_group[l], w_router_expert[l],
                         b_router_expert[l], w_gate[l], w_up[l], w_down[l])
    return x


def setup_inputs(seed=0):
    out = dict(first_inputs(seed))
    for name, value in second_inputs(seed + 1).items():
        if name != "x":
            out[name + "_2"] = value
    return out


def reference(
    x, c, ctx, c_ctx, ada_w, ada_b, norm_mix_g, norm_ffn_g, even_w_in, even_w_out,
    hgrn_lb_logits, hgrn_onorm_g, diff_lambda, diff_subln_g, odd_w_qkv, odd_w_out, swa_sink,
    router_w, router_b, moe_w_gate, moe_w_up, moe_w_down, final_norm_g, c_2, positions_2,
    w_ada_2, b_ada_2, norm1_g_2, w_in_2, q_a_norm_2, w_q_b_2, kv_a_norm_2, w_kv_b_2, q_norm_2,
    k_norm_2, conv_w_2, conv_b_2, lru_wa_2, lru_ba_2, lru_wx_2, lru_bx_2, lru_lambda_2,
    attn_out_norm_2, lru_out_norm_2, w_out_2, norm2_g_2, w_router_group_2, b_router_group_2,
    w_router_expert_2, b_router_expert_2, w_gate_2, w_up_2, w_down_2,
):
    x = first_block(
        x, c, ctx, c_ctx, ada_w, ada_b, norm_mix_g, norm_ffn_g, even_w_in, even_w_out,
        hgrn_lb_logits, hgrn_onorm_g, diff_lambda, diff_subln_g, odd_w_qkv, odd_w_out, swa_sink,
        router_w, router_b, moe_w_gate, moe_w_up, moe_w_down, final_norm_g,
    )
    return second_block(
        x, c_2, positions_2, w_ada_2, b_ada_2, norm1_g_2, w_in_2, q_a_norm_2, w_q_b_2,
        kv_a_norm_2, w_kv_b_2, q_norm_2, k_norm_2, conv_w_2, conv_b_2, lru_wa_2, lru_ba_2,
        lru_wx_2, lru_bx_2, lru_lambda_2, attn_out_norm_2, lru_out_norm_2, w_out_2, norm2_g_2,
        w_router_group_2, b_router_group_2, w_router_expert_2, b_router_expert_2, w_gate_2,
        w_up_2, w_down_2,
    )


_drawn_inputs = setup_inputs


def setup_inputs(seed=0):
    import zlib

    import numpy as np

    out = dict(_drawn_inputs(seed))
    spreads = {}
    factors = {'norm_mix_g': 2.769,
     'hgrn_lb_logits': 8.0,
     'hgrn_onorm_g': 4.229,
     'diff_subln_g': 3.317,
     'swa_sink': 64.0,
     'norm1_g_2': 3.122,
     'q_a_norm_2': 7.214,
     'kv_a_norm_2': 3.458,
     'q_norm_2': 8.0,
     'k_norm_2': 8.0,
     'lru_ba_2': 27.114,
     'lru_bx_2': 8.0,
     'attn_out_norm_2': 14.962,
     'lru_out_norm_2': 15.319,
     'b_router_group_2': 18.319,
     'b_router_expert_2': 27.913,
     'conv_b_2': 2.985,
     'norm2_g_2': 5.454}
    for name, (base, spread) in spreads.items():
        noise = np.random.default_rng([zlib.crc32(name.encode()), seed]).standard_normal(out[name].shape)
        drawn = base * np.exp(spread * noise) if base else spread * noise
        out[name] = __import__('jax').numpy.asarray(drawn.astype(out[name].dtype))
    for name, factor in factors.items():
        out[name] = (out[name] * factor).astype(out[name].dtype)
    return out
```

```python
import math
from contextlib import ExitStack, contextmanager

import numpy as np

import concourse.bass as bass
from concourse import mybir
from concourse.alu_op_type import AluOpType as ALU

F32 = mybir.dt.float32
I32 = mybir.dt.int32
U8 = mybir.dt.uint8
ACT = mybir.ActivationFunctionType
AX = mybir.AxisListType

P = 128
D = 1024
KT = D // P
EPS = 1e-6
NEG = -1e30
SLOT = 2048
RING = 6
CHUNK_COLS = SLOT // KT
CTX, LAT = (0, 1), (2, 3)
NTOK = 4 * P
LEVELS = (64, 32, 16, 8, 4, 2, 1)
CAP = (128, 64, 64)
TWO_PI = 2.0 * math.pi
LAMBDA_INIT = 0.8 - 0.6 * math.exp(-0.3 * 0)


class Counted:

    def __init__(self, sem):
        self.sem, self.base, self.given = sem, 0, 0

    def at(self, n):
        return self.base + n

    def up(self):
        self.given += 1
        return 1

    def last(self):
        return self.base + self.given


class Core:

    def __init__(self, nc, ctx):
        self.nc, self.ctx, self.semaphores, self.table = nc, ctx, [], {}
        self.chunks, self.issued, self.taken = [], 0, 0
        self.landed = [ctx.enter_context(nc.semaphore(f"weights_landed_{i}")) for i in range(RING)]
        self.released = self.counted("weights_released")

    def sb(self, name, shape, dtype=F32):
        return self.ctx.enter_context(self.nc.sbuf_tensor(name, shape, dtype))

    def col(self, name, n, at=0):
        a = self.columns_at[name] + at
        return self.COL[:, a:a + n]

    def counted(self, name):
        if name not in self.table:
            s = Counted(self.ctx.enter_context(self.nc.semaphore(name)))
            self.semaphores.append(s)
            self.table[name] = s
        return self.table[name]

    @contextmanager
    def phase(self, name):
        with self.nc.Block(no_gpsimd_drain=True) as block:
            yield block
        for s in self.semaphores:
            s.base, s.given = s.base + s.given, 0

    def slot(self, n, a, b):
        at = (n % RING) * SLOT
        return self.ring[:, at:at + a * b].rearrange("p (a b) -> p a b", a=a)

    def feed(self, sp, consumed):
        upto = min(self.fed_base + consumed + RING, len(self.chunks))
        for n in range(self.issued, upto):
            if n >= RING:
                sp.wait_ge(self.released.sem, n - RING + 1)
            src = self.chunks[n]
            sp.dma_start(self.slot(n, src.shape[1], src.shape[2]), src).then_inc(self.landed[n % RING], 16)
        self.issued = max(self.issued, upto)
        self.fed_base += consumed

    def take(self, pe):
        n = self.taken
        self.taken += 1
        pe.wait_ge(self.landed[n % RING], 16 * (n // RING + 1))
        return self.slot(n, self.chunks[n].shape[1], self.chunks[n].shape[2])

    fed_base = 0


def columns(w, c, width=CHUNK_COLS):
    return w[:, c * CHUNK_COLS:c * CHUNK_COLS + width].rearrange("(k p) n -> p k n", p=P)


def products(pe, out, pairs, first=True, last=True):
    for i, (left, right) in enumerate(pairs):
        ins = pe.matmul(out, left, right, start=first and i == 0, stop=last and i == len(pairs) - 1,
                        skip_group_check=True)
    return ins


def project(K, name, n_chunks, outs, product, drain, engine=lambda c, o: "v", banks=8):
    filled, released = K.counted("bank_filled"), K.released
    drained = [K.counted(f"bank_{b}_drained") for b in range(banks)]
    with K.phase(name) as block:
        @block.sync
        def _(sp):
            K.feed(sp, n_chunks)

        @block.tensor
        def _(pe):
            for c in range(n_chunks):
                w = K.take(pe)
                for o in range(outs):
                    j = c * outs + o
                    if j >= banks:
                        pe.wait_ge(drained[j % banks].sem, drained[j % banks].at(j // banks))
                    ins = product(pe, w, K.PS[:, j % banks, :], c, o)
                    done = released if o == outs - 1 else filled
                    ins.then_inc(done.sem, done.up())

        def drains(eng, which):
            for j in range(n_chunks * outs):
                c, o = j // outs, j % outs
                if engine(c, o) == which:
                    if o == outs - 1:
                        eng.wait_ge(released.sem, released.at(c + 1))
                    else:
                        eng.wait_ge(filled.sem, filled.at(c * (outs - 1) + o + 1))
                    drain(eng, K.PS[:, j % banks, :], c, o).then_inc(drained[j % banks].sem, drained[j % banks].up())

        @block.vector
        def _(v):
            drains(v, "v")

        @block.scalar
        def _(act):
            drains(act, "a")


def load_constants(K, A, C):
    loads = K.counted("vectors_transposed")
    small = K.ctx.enter_context(K.nc.semaphore("small_loaded"))
    count = [0]
    with K.phase("constants") as block:
        @block.sync
        def _(sp):
            def load(dst, src):
                sp.dma_start(dst, src).then_inc(small, 16)
                count[0] += 16
            load(K.IDENT[:, :], C["c_ident"])
            load(K.MASKS32, C["c_masks"])
            load(K.ROPE[:, :, :], C["c_rope"].rearrange("(t p) n -> p t n", p=P))
            load(K.BAND[:, :, :], C["c_band"].rearrange("(t p) n -> p t n", p=P))
            load(K.CAUSAL[:, :], C["c_causal"])
            load(K.STRICT[:, :], C["c_strict"])
            load(K.BEFORE[:, :], C["c_before"])
            load(K.IOTA[:, :], C["c_iota"].partition_broadcast(P))
            load(K.INV[:, :], C["c_inv"].partition_broadcast(P))
            K.columns_at = {}
            row = 0
            for name, src in K.vectors:
                n = src.shape[0]
                K.columns_at[name] = row
                done = 0
                while done < n:
                    tile, at = divmod(row + done, P)
                    m = min(n - done, P - at)
                    load(K.VROW[at:at + m, tile, :], src[done:done + m, :])
                    done += m
                row += n
            K.n_rows = row
            load(K.X[:, 0:2, :], A["ctx"][0].rearrange("(t p) d -> p t d", p=P))
            load(K.X[:, 2:4, :], A["x"][0].rearrange("(t p) d -> p t d", p=P))
            load(K.DLAM[:, :], A["diff_lambda"].rearrange("a b c -> (a b c)").partition_broadcast(P))
            load(K.SINK[:, :], A["swa_sink"].rearrange("a b -> (a b)").partition_broadcast(P))
            load(K.QKN[:, 0, :], A["q_norm_2"].rearrange("a b -> (a b)").partition_broadcast(P))
            load(K.QKN[:, 1, :], A["k_norm_2"].rearrange("a b -> (a b)").partition_broadcast(P))
            load(K.ROUT[:, :, 0:16], A["router_w"].rearrange("(k p) n -> p k n", p=P))
            load(K.ROUT[:, :, 16:20], A["w_router_group_2"][0].rearrange("(k p) n -> p k n", p=P))
            load(K.ROUT[:, :, 20:52], A["w_router_expert_2"][0].rearrange("(k p) n -> p k n", p=P))
            load(K.RB[:, 0:16], A["router_b"].partition_broadcast(P))
            load(K.RB[:, 16:20], A["b_router_group_2"].rearrange("a b -> (a b)").partition_broadcast(P))
            load(K.RB[:, 20:52], A["b_router_expert_2"].rearrange("a b -> (a b)").partition_broadcast(P))
            for t in range(2):
                load(K.POSI[:, t:t + 1], A["positions_2"][0, t * P:t * P + P].rearrange("(p o) -> p o", o=1))
            load(K.POSR[:, :], A["positions_2"].rearrange("a b -> (a b)").partition_broadcast(P))
            K.feed(sp, 0)
            sp.wait_ge(small, count[0])

        @block.vector
        def _(v):
            v.memset(K.ONES[:, :], 1.0)

    tiles = -(-K.n_rows // P)
    with K.phase("vectors to columns") as block:
        @block.tensor
        def _(pe):
            for t in range(tiles):
                n = min(P, K.n_rows - t * P)
                ins = pe.transpose(K.PS[:, 0, t * P:t * P + n], K.VROW[0:n, t, :], K.IDENT[0:n, 0:n])
            ins.then_inc(loads.sem, loads.up())

        @block.vector
        def _(v):
            v.tensor_copy(K.MASKS[:, :, :], K.MASKS32)
            v.wait_ge(loads.sem, loads.at(1))
            v.tensor_copy(K.COL[:, 0:K.n_rows], K.PS[:, 0, 0:K.n_rows])

    less, exps = K.counted("logits_ready"), K.counted("exponentials_ready")
    with K.phase("silu of the conditioning vectors, lambda, lower bounds") as block:
        @block.scalar
        def _(act):
            for i, name in enumerate(("c", "c_ctx", "c_2")):
                act.activation(K.CS[:, :, i], K.col(name, KT), ACT.Silu)
            act.wait_ge(less.sem, less.at(1))
            act.activation(K.DL[:, 0:2], K.DL[:, 0:2], ACT.Exp).then_inc(exps.sem, exps.up())
            act.wait_ge(less.sem, less.at(2))
            act.activation(K.LB[:, 0:3, :], K.LB[:, 0:3, :], ACT.Exp).then_inc(exps.sem, exps.up())

        @block.vector
        def _(v):
            own = K.counted("vector_step")
            pairs = K.DLAM[:, :].rearrange("p (a b c) -> p a b c", a=2, b=2)
            dots = K.DL[:, 128:256].rearrange("p (a b) -> p a b", a=2)
            v.tensor_tensor(dots, pairs[:, :, 0, :], pairs[:, :, 1, :], ALU.mult).then_inc(own.sem, own.up())
            v.wait_ge(own.sem, own.last())
            v.tensor_reduce(K.DL[:, 0:2], dots, AX.X, ALU.add).then_inc(less.sem, less.up())
            lb = K.col("lb", 24).rearrange("p (l n) -> p l n", l=3)
            v.tensor_tensor(K.LB[:, 3, :], lb[:, 0, :], lb[:, 1, :], ALU.max).then_inc(own.sem, own.up())
            v.wait_ge(own.sem, own.last())
            v.tensor_tensor(K.LB[:, 3, :], K.LB[:, 3, :], lb[:, 2, :], ALU.max).then_inc(own.sem, own.up())
            v.wait_ge(own.sem, own.last())
            ins = v.tensor_tensor(K.LB[:, 0:3, :], lb, K.LB[:, 3:4, :].to_broadcast([P, 3, 8]), ALU.subtract)
            ins.then_inc(less.sem, less.up())
            v.wait_ge(exps.sem, exps.at(2))
            v.tensor_tensor(K.LB[:, 3, :], K.LB[:, 0, :], K.LB[:, 1, :], ALU.add).then_inc(own.sem, own.up())
            v.wait_ge(own.sem, own.last())
            v.tensor_tensor(K.LB[:, 3, :], K.LB[:, 3, :], K.LB[:, 2, :], ALU.add).then_inc(own.sem, own.up())
            v.wait_ge(own.sem, own.last())
            v.reciprocal(K.LB[:, 3, :], K.LB[:, 3, :]).then_inc(own.sem, own.up())
            v.wait_ge(own.sem, own.last())
            v.tensor_tensor(K.LB[:, 0, :], K.LB[:, 0, :], K.LB[:, 3, :], ALU.mult).then_inc(own.sem, own.up())
            v.wait_ge(own.sem, own.last())
            v.tensor_scalar(K.LB[:, 1, :], K.LB[:, 0, :], -1.0, 1.0, ALU.mult, ALU.add).then_inc(own.sem, own.up())
            v.wait_ge(own.sem, own.last())
            v.tensor_tensor(K.DL[:, 2:3], K.DL[:, 1:2], K.DL[:, 0:1], ALU.subtract).then_inc(own.sem, own.up())
            v.wait_ge(own.sem, own.last())
            v.tensor_scalar(K.DL[:, 2:3], K.DL[:, 2:3], -LAMBDA_INIT, None, ALU.add).then_inc(own.sem, own.up())
            v.wait_ge(own.sem, own.last())
            ins = v.tensor_scalar(K.SUBLN[:, :], K.col("subln", 1), 1.0 - LAMBDA_INIT, None, ALU.mult)
            ins.then_inc(own.sem, own.up())
            v.wait_ge(own.sem, own.last())


def modulation(K, bias, streams, gain1, gain2):
    n = len(streams)

    def product(pe, w, bank, c, o):
        for f in range(2):
            ins = products(pe, bank[:, f * n:f * n + n],
                           [(w[:, k, f * P:f * P + P], K.CS[:, k, streams[0]:streams[0] + n]) for k in range(KT)])
        return ins

    def drain(v, bank, c, o):
        at = K.columns_at[bias] + 2 * c
        b = K.COL[:, at:at + 2].rearrange("p (f o) -> p f o", o=1).to_broadcast([P, 2, n])
        return v.tensor_tensor(K.MOD[:, 2 * c:2 * c + 2, 0:n],
                               bank[:, 0:2 * n].rearrange("p (f s) -> p f s", f=2), b, ALU.add)

    project(K, "modulation", 24, 1, product, drain)
    own = K.counted("vector_step")
    with K.phase("affine") as block:
        @block.vector
        def _(v):
            for i, (sec, gain) in enumerate(((1, gain1), (4, gain2))):
                for s in range(n):
                    ins = v.tensor_scalar(K.AFF[:, i, :, s], K.MOD[:, 8 * sec:8 * sec + 8, s], 1.0, None, ALU.add)
                    ins.then_inc(own.sem, own.up())
                    v.wait_ge(own.sem, own.last())
                    ins = v.tensor_tensor(K.AFF[:, i, :, s], K.AFF[:, i, :, s], K.col(gain, KT), ALU.mult)
                    ins.then_inc(own.sem, own.up())
                    v.wait_ge(own.sem, own.last())


def normalise(K, tiles, width, source, scaled, groups=1):
    own, sums, root = K.counted("vector_step"), K.counted("square_sums"), K.counted("roots")
    n = len(tiles) * groups
    with K.phase("normalise") as block:
        @block.vector
        def _(v):
            for i, t in enumerate(tiles):
                sq = K.SQ[:, 0:groups * width].rearrange("p (g w) -> p g w", g=groups)
                v.tensor_tensor(sq, source(t), source(t), ALU.mult).then_inc(own.sem, own.up())
                v.wait_ge(own.sem, own.last())
                v.tensor_reduce(K.STAT[:, i * groups:(i + 1) * groups], sq, AX.X, ALU.add).then_inc(own.sem, own.up())
                v.wait_ge(own.sem, own.last())
            ins = v.tensor_scalar(K.STAT[:, 0:n], K.STAT[:, 0:n], 1.0 / width, EPS, ALU.mult, ALU.add)
            ins.then_inc(sums.sem, sums.up())
            v.wait_ge(root.sem, root.at(1))
            v.reciprocal(K.STAT[:, 0:n], K.STAT[:, 0:n]).then_inc(own.sem, own.up())
            v.wait_ge(own.sem, own.last())
            for i, t in enumerate(tiles):
                r = K.STAT[:, i * groups:(i + 1) * groups].rearrange("p (g o) -> p g o", o=1)
                v.tensor_tensor(scaled(t), source(t), r.to_broadcast([P, groups, width]), ALU.mult)

        @block.scalar
        def _(act):
            act.wait_ge(sums.sem, sums.at(1))
            act.activation(K.STAT[:, 0:n], K.STAT[:, 0:n], ACT.Sqrt).then_inc(root.sem, root.up())


def turn(K, tiles, n, source, drain, banks=8):
    filled = K.counted("bank_filled")
    drained = [K.counted(f"bank_{b}_drained") for b in range(banks)]
    with K.phase("turn") as block:
        @block.tensor
        def _(pe):
            for k in range(n):
                if k >= banks:
                    pe.wait_ge(drained[k % banks].sem, drained[k % banks].at(k // banks))
                for i, t in enumerate(tiles):
                    src = source(t, k)
                    m = src.shape[-1]
                    ins = pe.transpose(K.PS[0:m, k % banks, i * P:i * P + P], src, K.IDENT[:, :])
                ins.then_inc(filled.sem, filled.up())

        def drains(eng, odd):
            for k in range(odd, n, 2):
                eng.wait_ge(filled.sem, filled.at(k + 1))
                drain(eng, K.PS[:, k % banks, :], k).then_inc(drained[k % banks].sem, drained[k % banks].up())

        @block.vector
        def _(v):
            drains(v, 0)

        @block.scalar
        def _(act):
            drains(act, 1)


def affine(K, eng, out, src, scale, bias):
    if eng.engine == K.nc.vector.engine:
        return eng.tensor_scalar(out, src, scale, bias, ALU.mult, ALU.add)
    return eng.activation(out, src, ACT.Identity, bias=bias, scale=scale)


def scaled_copy(K, eng, out, src, scale):
    if eng.engine == K.nc.vector.engine:
        return eng.tensor_scalar(out, src, scale, None, ALU.mult)
    return eng.activation(out, src, ACT.Copy, scale=scale)


def copy(K, eng, out, src):
    if eng.engine == K.nc.vector.engine:
        return eng.tensor_copy(out, src)
    return eng.activation(out, src, ACT.Copy)


def modulated(K, which, tiles, HT):
    shift = 8 * (0 if which == 0 else 3)
    normalise(K, tiles, D, lambda t: K.X[:, t:t + 1, :], lambda t: K.YN[:, t:t + 1, :])

    def drain(eng, bank, k):
        runs = [(0, 0, 2, 1), (2, 2, 4, 0)] if len(tiles) == 4 else [(0, 2, 4, 0)]
        for at, a, b, s in runs:
            ins = affine(K, eng, HT[:, k, a * P:b * P], bank[:, at * P:(at + b - a) * P],
                         K.AFF[:, which, k, s:s + 1], K.MOD[:, shift + k, s:s + 1])
        return ins

    turn(K, tiles, KT, lambda t, k: K.YN[:, t, k * P:k * P + P], drain)


def spread(K, source, out):
    diag, own = K.counted("diagonals"), K.counted("bank_filled")
    with K.phase("spread") as block:
        @block.vector
        def _(v):
            for k in range(KT):
                ins = v.tensor_scalar(K.SQ[:, k * P:k * P + P], K.IDENT[:, :], source(k), None, ALU.mult)
                ins.then_inc(diag.sem, diag.up())
            for b in range(2):
                v.wait_ge(own.sem, own.at(b + 1))
                v.tensor_copy(out[:, b * 512:b * 512 + 512], K.PS[:, b, :])

        @block.tensor
        def _(pe):
            for k in range(KT):
                pe.wait_ge(diag.sem, diag.at(k + 1))
                ins = pe.matmul(K.PS[:, k // 4, (k % 4) * P:(k % 4) * P + P], K.ONES[:, :],
                                K.SQ[:, k * P:k * P + P], start=True, stop=True, skip_group_check=True)
                if k % 4 == 3:
                    ins.then_inc(own.sem, own.up())


def gated_residual(K, tiles, YT, section):
    streams = (0, 1) if len(tiles) == 4 else (0,)
    for s in streams:
        spread(K, lambda k, s=s: K.MOD[:, 8 * section + k, s:s + 1], K.GB[:, s, :])
    own = K.counted("vector_step")

    def product(pe, w, bank, c, o):
        t = tiles[o]
        return products(pe, bank[:, 0:CHUNK_COLS], [(YT[:, k, t * P:t * P + P], w[:, k, :]) for k in range(KT)])

    def drain(v, bank, c, o):
        t = tiles[o]
        s = 1 if t in CTX else 0
        cols = slice(c * CHUNK_COLS, (c + 1) * CHUNK_COLS)
        half = (c * len(tiles) + o) % 2
        tmp = K.SQ[:, half * CHUNK_COLS:(half + 1) * CHUNK_COLS]
        v.tensor_tensor(tmp, bank[:, 0:CHUNK_COLS], K.GB[:, s, cols], ALU.mult).then_inc(own.sem, own.up())
        v.wait_ge(own.sem, own.last())
        return v.tensor_tensor(K.X[:, t, cols], K.X[:, t, cols], tmp, ALU.add)

    project(K, "output projection", 4, len(tiles), product, drain)


def attention(K, units, finish_every, finish):
    scored, turned, summed = K.counted("scores_ready"), K.counted("weights_turned"), K.counted("outputs_ready")
    masked, exped = K.counted("logits_ready"), K.counted("exponentials_ready")
    combined, copied, taken = K.counted("weights_ready"), K.counted("turned_copied"), K.counted("outputs_taken")
    own, asum = K.counted("vector_step"), K.counted("scalar_step")
    n = len(units)
    with K.phase("attention") as block:
        @block.tensor
        def _(pe):
            def scores(u):
                if u >= 2:
                    pe.wait_ge(exped.sem, exped.at(u - 1))
                for m, pairs in enumerate(units[u]["scores"]):
                    ins = products(pe, K.PS[:, 2 * (u % 2) + m, 0:units[u]["nk"]], pairs)
                ins.then_inc(scored.sem, scored.up())

            scores(0)
            for u in range(n):
                if u + 1 < n:
                    scores(u + 1)
                nt = units[u]["nk"] // P
                pe.wait_ge(combined.sem, combined.at(u + 1))
                if u >= 2:
                    pe.wait_ge(copied.sem, copied.at(u - 1))
                for i in range(nt):
                    ins = pe.transpose(K.PS[:, 4 + u % 2, i * P:i * P + P], K.AW[:, u % 2, i * P:i * P + P],
                                       K.IDENT[:, :])
                ins.then_inc(turned.sem, turned.up())
                if u % finish_every == 0 and u >= 2 * finish_every:
                    pe.wait_ge(taken.sem, taken.at(u // finish_every - 1))
                pe.wait_ge(copied.sem, copied.at(u + 1))
                bank = K.PS[:, 6 + (u // finish_every) % 2, :]
                ins = products(pe, units[u]["out"](bank),
                               [(K.AWT[:, u % 2, i * P:i * P + P], units[u]["values"](i)) for i in range(nt)])
                ins.then_inc(summed.sem, summed.up())

        @block.vector
        def _(v):
            def softmax_in(u):
                unit, nk, s = units[u], units[u]["nk"], u % 2
                v.wait_ge(scored.sem, scored.at(u + 1))
                if u >= 2:
                    v.wait_ge(exped.sem, exped.at(u - 1))
                for m in range(len(unit["scores"])):
                    src = K.PS[:, 2 * s + m, 0:nk]
                    if unit["mask"] is not None:
                        ins = v.scalar_tensor_tensor(K.LG[:, s, 0:nk], src, unit["scale"], unit["mask"],
                                                     ALU.mult, ALU.add)
                        ins.then_inc(own.sem, own.up())
                        v.wait_ge(own.sem, own.last())
                        src = K.LG[:, s, 0:nk]
                    v.tensor_reduce(K.MX[:, s, m:m + 1], src, AX.X, ALU.max).then_inc(own.sem, own.up())
                    v.wait_ge(own.sem, own.last())
                    sc = 1.0 if unit["mask"] is not None else unit["scale"]
                    if unit["sink"] is not None:
                        ins = v.tensor_scalar(K.MX[:, s, m:m + 1], K.MX[:, s, m:m + 1], sc, unit["sink"],
                                              ALU.mult, ALU.max)
                        ins.then_inc(own.sem, own.up())
                        v.wait_ge(own.sem, own.last())
                        sc = 1.0
                    ins = v.tensor_scalar(K.MX[:, s, 2 + m:3 + m], K.MX[:, s, m:m + 1], -sc, None, ALU.mult)
                    if m < len(unit["scores"]) - 1:
                        ins.then_inc(own.sem, own.up())
                        v.wait_ge(own.sem, own.last())
                ins.then_inc(masked.sem, masked.up())

            softmax_in(0)
            for u in range(n):
                if u + 1 < n:
                    softmax_in(u + 1)
                unit, nk, s = units[u], units[u]["nk"], u % 2
                v.wait_ge(exped.sem, exped.at(u + 1))
                if u >= 2:
                    v.wait_ge(turned.sem, turned.at(u - 1))
                maps = len(unit["scores"])
                if unit["sink"] is not None:
                    ins = v.tensor_tensor(K.MX[:, s, 4:5], K.MX[:, s, 4:5], K.MX[:, s, 5:6], ALU.add)
                    ins.then_inc(own.sem, own.up())
                    v.wait_ge(own.sem, own.last())
                v.reciprocal(K.MX[:, s, 6:6 + maps], K.MX[:, s, 4:4 + maps]).then_inc(own.sem, own.up())
                v.wait_ge(own.sem, own.last())
                if maps == 1:
                    ins = v.tensor_scalar(K.AW[:, s, 0:nk], K.EX[:, s, 0, 0:nk], K.MX[:, s, 6:7], None,
                                          ALU.mult)
                    ins.then_inc(combined.sem, combined.up())
                else:
                    ins = v.tensor_tensor(K.MX[:, s, 7:8], K.MX[:, s, 7:8], K.DL[:, 2:3], ALU.mult)
                    ins.then_inc(own.sem, own.up())
                    v.wait_ge(own.sem, own.last())
                    ins = v.tensor_scalar(K.AW[:, s, 0:nk], K.EX[:, s, 0, 0:nk], K.MX[:, s, 6:7], None,
                                          ALU.mult)
                    ins.then_inc(own.sem, own.up())
                    v.wait_ge(own.sem, own.last())
                    ins = v.scalar_tensor_tensor(K.AW[:, s, 0:nk], K.EX[:, s, 1, 0:nk], K.MX[:, s, 7:8],
                                                 K.AW[:, s, 0:nk], ALU.mult, ALU.add)
                    ins.then_inc(combined.sem, combined.up())
                if u % finish_every == 0 and u:
                    v.wait_ge(summed.sem, summed.at(u))
                    i = u // finish_every - 1
                    finish(v, K.PS[:, 6 + i % 2, :], i).then_inc(taken.sem, taken.up())
            v.wait_ge(summed.sem, summed.at(n))
            i = n // finish_every - 1
            finish(v, K.PS[:, 6 + i % 2, :], i).then_inc(taken.sem, taken.up())

        @block.scalar
        def _(act):
            def exponentials(u):
                unit, nk, s = units[u], units[u]["nk"], u % 2
                act.wait_ge(masked.sem, masked.at(u + 1))
                if u >= 2:
                    act.wait_ge(combined.sem, combined.at(u - 1))
                if unit["sink"] is not None:
                    act.activation(K.MX[:, s, 5:6], unit["sink"], ACT.Exp, bias=K.MX[:, s, 2:3])
                for m in range(len(unit["scores"])):
                    src, sc = ((K.LG[:, s, 0:nk], 1.0) if unit["mask"] is not None else
                               (K.PS[:, 2 * s + m, 0:nk], unit["scale"]))
                    ins = act.activation(K.EX[:, s, m, 0:nk], src, ACT.Exp, bias=K.MX[:, s, 2 + m:3 + m],
                                         scale=sc, accum_out=K.MX[:, s, 4 + m:5 + m])
                ins.then_inc(exped.sem, exped.up())

            exponentials(0)
            for u in range(n):
                if u + 1 < n:
                    exponentials(u + 1)
                act.wait_ge(turned.sem, turned.at(u + 1))
                if u >= 2:
                    act.wait_ge(summed.sem, summed.at(u - 1))
                nk = units[u]["nk"]
                ins = act.activation(K.AWT[:, u % 2, 0:nk], K.PS[:, 4 + u % 2, 0:nk], ACT.Copy)
                ins.then_inc(copied.sem, copied.up())


def rotate(K, tiles, x, table, tmp):
    own = K.counted("vector_step")
    with K.phase("rotary") as block:
        @block.vector
        def _(v):
            for t in tiles:
                a = x(t)
                n = a.shape[1]
                cos, sin = (z.rearrange("p (o w) -> p o w", o=1).to_broadcast([P, n, 64]) for z in table(t))
                sw = tmp[:, 0:n * 64].rearrange("p (h w) -> p h w", h=n)
                v.tensor_copy(sw[:, :, 0:32], a[:, :, 32:64])
                v.tensor_copy(sw[:, :, 32:64], a[:, :, 0:32]).then_inc(own.sem, own.up())
                v.wait_ge(own.sem, own.last())
                v.tensor_tensor(sw, sw, sin, ALU.mult).then_inc(own.sem, own.up())
                v.wait_ge(own.sem, own.last())
                v.tensor_tensor(a, a, cos, ALU.mult).then_inc(own.sem, own.up())
                v.wait_ge(own.sem, own.last())
                v.tensor_tensor(a, a, sw, ALU.add).then_inc(own.sem, own.up())
                v.wait_ge(own.sem, own.last())


def axial(K, tiles, x, heads):
    own = K.counted("vector_step")
    with K.phase("axial rotary") as block:
        @block.vector
        def _(v):
            for t in tiles:
                cos = K.ROPE[:, t - 2, 0:64].rearrange("p (o w) -> p o w", o=1).to_broadcast([P, heads, 64])
                sin = K.ROPE[:, t - 2, 64:128].rearrange("p (o w) -> p o w", o=1).to_broadcast([P, heads, 64])
                a = x(t).rearrange("p (h w) -> p h w", h=heads)
                sw = K.SQ[:, 0:heads * 64].rearrange("p (h w) -> p h w", h=heads)
                a4 = x(t).rearrange("p (g s w) -> p g s w", s=2, w=16)
                s4 = K.SQ[:, 0:heads * 64].rearrange("p (g s w) -> p g s w", s=2, w=16)
                v.tensor_copy(s4[:, :, 0, :], a4[:, :, 1, :])
                v.tensor_copy(s4[:, :, 1, :], a4[:, :, 0, :]).then_inc(own.sem, own.up())
                v.wait_ge(own.sem, own.last())
                v.tensor_tensor(sw, sw, sin, ALU.mult).then_inc(own.sem, own.up())
                v.wait_ge(own.sem, own.last())
                v.tensor_tensor(a, a, cos, ALU.mult).then_inc(own.sem, own.up())
                v.wait_ge(own.sem, own.last())
                v.tensor_tensor(a, a, sw, ALU.add).then_inc(own.sem, own.up())
                v.wait_ge(own.sem, own.last())


def turned_output(K, tiles, n, source, gain, dst):
    def drain(eng, bank, k):
        return scaled_copy(K, eng, dst(k), bank[:, 0:len(tiles) * P], gain(k))
    turn(K, tiles, n, source, drain)


def diff_attention(K, A, HT, YT):
    TM, VA, QK = K.YN, K.VB, K.FM

    def product(pe, w, bank, c, t):
        return products(pe, bank[:, 0:CHUNK_COLS], [(HT[:, k, t * P:t * P + P], w[:, k, :]) for k in range(KT)])

    def drain(eng, bank, c, t):
        dst = TM[:, t, c * 256:c * 256 + 256] if c < 4 else VA[:, t, (c - 4) * 256:(c - 3) * 256]
        return copy(K, eng, dst, bank[:, 0:CHUNK_COLS])

    project(K, "differential q, k, v", 6, 4, product, drain, engine=lambda c, o: "va"[o % 2])
    axial(K, LAT, lambda t: TM[:, t, :], 16)
    turn(K, (0, 1, 2, 3), 8, lambda t, k: TM[:, t, k * P:k * P + P],
         lambda eng, bank, k: copy(K, eng, QK[:, k, :], bank))
    units = []
    for t in range(4):
        nk = 256 if t in CTX else 512
        for h in range(4):
            units.append(dict(
                nk=nk, scale=64 ** -0.5, mask=None, sink=None,
                scores=[[(QK[64 * m:64 * m + 64, h, t * P:t * P + P], QK[64 * m:64 * m + 64, 4 + h, 0:nk])]
                        for m in range(2)],
                values=lambda i, h=h: VA[:, i, h * P:h * P + P],
                out=lambda bank, h=h: bank[:, h * P:h * P + P]))
    attention(K, units, 4, lambda v, bank, i: v.tensor_copy(TM[:, i, 0:512], bank))
    heads = lambda t: TM[:, t, 0:512].rearrange("p (h w) -> p h w", h=4)
    normalise(K, (0, 1, 2, 3), P, heads, heads, groups=4)
    turned_output(K, (0, 1, 2, 3), 4, lambda t, k: TM[:, t, k * P:k * P + P],
                  lambda k: K.SUBLN[:, 0:1], lambda k: YT[:, 4 + k, :])


def hgrn2(K, A, HT, YT):
    Q, KK, LF, VA, GA = K.FM[:, 0:4, :], K.BIG, K.LF, K.VB, K.GA
    own, act_own = K.counted("vector_step"), K.counted("scalar_step")

    def product(pe, w, bank, c, o):
        if c < 6:
            return products(pe, bank, [(w[:, k, o * P:o * P + P], HT[:, k, :]) for k in range(KT)])
        ins = None
        for i in range(2):
            t = 2 * o + i
            ins = products(pe, bank[:, i * 256:i * 256 + 256],
                           [(HT[:, k, t * P:t * P + P], w[:, k, :]) for k in range(KT)])
        return ins

    def drain(eng, bank, c, o):
        if c < 2:
            return eng.activation(Q[:, 2 * c + o, :], bank, ACT.Silu)
        if c < 6:
            return eng.activation(LF[:, 2 * (c - 2) + o, :], bank, ACT.Sigmoid)
        view = bank.rearrange("p (t n) -> p t n", t=2)
        if c < 8:
            return eng.tensor_copy(VA[:, 2 * o:2 * o + 2, (c - 6) * 256:(c - 5) * 256], view)
        return eng.activation(GA[:, 2 * o:2 * o + 2, (c - 8) * 256:(c - 7) * 256], view, ACT.Silu)

    project(K, "HGRN2 projections", 10, 2, product, drain, engine=lambda c, o: "v" if 6 <= c < 8 else "a")
    ready, logs = K.counted("gates_ready"), K.counted("logs_ready")
    with K.phase("gates") as block:
        @block.vector
        def _(v):
            v.tensor_scalar(Q, Q, float(P) ** -0.5, None, ALU.mult)
            for j in range(8):
                ins = v.tensor_scalar(LF[:, j, :], LF[:, j, :], K.LB[:, 1, j:j + 1], K.LB[:, 0, j:j + 1],
                                      ALU.mult, ALU.add)
                ins.then_inc(ready.sem, ready.up())
                v.wait_ge(ready.sem, ready.last())
                ins = v.tensor_scalar(KK[:, j, :], LF[:, j, :], -1.0, 1.0, ALU.mult, ALU.add)
                ins.then_inc(ready.sem, ready.up())
            for j in range(8):
                v.wait_ge(logs.sem, logs.at(j + 1))
                for b in range(4):
                    x = LF[:, j, b * P:b * P + P] if j < 4 else LF[:, j, b * P:b * P + P][:, ::-1]
                    v.tensor_tensor_scan(x, K.ONES[:, :], x, 0.0, ALU.mult, ALU.add)

        @block.scalar
        def _(act):
            for j in range(8):
                act.wait_ge(ready.sem, ready.at(2 * j + 2))
                act.activation(LF[:, j, :], LF[:, j, :], ACT.Ln).then_inc(logs.sem, logs.up())

    orders = ((0, 1, 2, 3), (1, 0, 3, 2))
    W0, W1, W2 = K.HW[:, 0, 0:512], K.HW[:, 1, 0:512], K.HW[:, 2, 0:512]
    h4 = lambda a: a.rearrange("p (h t) -> p h t", h=4)
    decayed, turned, copied = K.counted("keys_decayed"), K.counted("weights_turned"), K.counted("turned_copied")
    summed, diffs, expd = K.counted("outputs_ready"), K.counted("differences_ready"), K.counted("exponentials_ready")
    steps = [(i, d) for i in range(3) for d in range(2)]
    with K.phase("HGRN2 states") as block:
        @block.vector
        def _(v):
            for n, (i, d) in enumerate(steps):
                b = orders[d][i]
                cum = LF[:, 4 * d:4 * d + 4, b * P:b * P + P]
                total = cum[:, :, P - 1:P] if d == 0 else cum[:, :, 0:1]
                if n:
                    v.wait_ge(expd.sem, expd.at(2 * n))
                v.tensor_copy(K.TOT[:, d, :].rearrange("p (h o) -> p h o", o=1), total)
                ins = v.tensor_tensor(h4(W0), total.to_broadcast([P, 4, P]), cum, ALU.subtract)
                ins.then_inc(diffs.sem, diffs.up())
                v.wait_ge(expd.sem, expd.at(2 * n + 2))
                ins = v.tensor_tensor(h4(W1), KK[:, 4 * d:4 * d + 4, b * P:b * P + P], h4(W0), ALU.mult)
                ins.then_inc(decayed.sem, decayed.up())
                v.wait_ge(turned.sem, turned.at(n + 1))
                v.tensor_copy(W2, K.PS[:, 0, :]).then_inc(copied.sem, copied.up())
                v.wait_ge(summed.sem, summed.at(n + 1))
                if i == 0:
                    ins = v.tensor_copy(K.ST[:, d, 0, :], K.PS[:, 1, :])
                else:
                    for h in range(4):
                        ins = v.scalar_tensor_tensor(
                            K.ST[:, d, i, h * P:h * P + P], K.ST[:, d, i - 1, h * P:h * P + P],
                            K.TOT[:, d, h:h + 1], K.PS[:, 1, h * P:h * P + P], ALU.mult, ALU.add)
                ins.then_inc(own.sem, own.up())
                v.wait_ge(own.sem, own.last())

        @block.scalar
        def _(act):
            for n, (i, d) in enumerate(steps):
                act.wait_ge(diffs.sem, diffs.at(n + 1))
                act.activation(W0, W0, ACT.Exp).then_inc(expd.sem, expd.up())
                act.activation(K.TOT[:, d, :], K.TOT[:, d, :], ACT.Exp).then_inc(expd.sem, expd.up())

        @block.tensor
        def _(pe):
            for n, (i, d) in enumerate(steps):
                b = orders[d][i]
                pe.wait_ge(decayed.sem, decayed.at(n + 1))
                for h in range(4):
                    ins = pe.transpose(K.PS[:, 0, h * P:h * P + P], W1[:, h * P:h * P + P], K.IDENT[:, :])
                ins.then_inc(turned.sem, turned.up())
                pe.wait_ge(copied.sem, copied.at(n + 1))
                for h in range(4):
                    ins = pe.matmul(K.PS[:, 1, h * P:h * P + P], W2[:, h * P:h * P + P],
                                    VA[:, b, h * P:h * P + P], start=True, stop=True)
                ins.then_inc(summed.sem, summed.up())

    scored, placed, qk = K.counted("scores_ready"), K.counted("scores_placed"), K.counted("factors_ready")
    pkey, absd, taken = K.counted("keys_factored"), K.counted("absolutes_ready"), K.counted("outputs_taken")
    rounds = [(b, d, l) for b in range(4) for l in range(-1, len(LEVELS)) for d in range(2)]

    with K.phase("HGRN2 outputs") as block:
        @block.vector
        def _(v):
            def place(n):
                b, d, l = rounds[n]
                if l == -1 and d == 0:
                    return
                v.wait_ge(scored.sem, scored.at(n + 1))
                mask = K.MASKS[:, 0 if l == -1 else 1 + 2 * l + d, :].rearrange("p (o t) -> p o t", o=1)
                ins = v.copy_predicated(h4(K.HA[:, b % 2, :]), mask.to_broadcast([P, 4, P]), h4(K.PS[:, n % 4, :]))
                ins.then_inc(placed.sem, placed.up())

            def output(b):
                v.wait_ge(summed.sem, summed.at(b + 1))
                v.tensor_copy(K.OUTB[:, b, :], K.PS[:, 6 + b % 2, :]).then_inc(taken.sem, taken.up())

            v.memset(K.HA[:, :, :], 0.0).then_inc(own.sem, own.up())
            v.wait_ge(own.sem, own.last())
            for n, (b, d, l) in enumerate(rounds):
                s = n % 2
                cum = LF[:, 4 * d:4 * d + 4, b * P:b * P + P]
                q = Q[:, :, b * P:b * P + P]
                key = KK[:, 4 * d:4 * d + 4, b * P:b * P + P]
                if n >= 2:
                    v.wait_ge(scored.sem, scored.at(n - 1))
                    v.wait_ge(qk.sem, qk.at(n - 1))
                if l >= 0:
                    w = 2 * LEVELS[l]
                    at = LEVELS[l] - 1 if d == 0 else LEVELS[l]
                    cv = cum.rearrange("p h (g w) -> p h g w", w=w)
                    ev = h4(K.HW[:, s, :]).rearrange("p h (g w) -> p h g w", w=w)
                    ins = v.tensor_tensor(ev, cv, cv[:, :, :, at:at + 1].to_broadcast([P, 4, P // w, w]),
                                          ALU.subtract)
                    ins.then_inc(diffs.sem, diffs.up())
                else:
                    v.tensor_copy(h4(K.HW[:, s, :]), cum).then_inc(diffs.sem, diffs.up())
                if n:
                    place(n - 1)
                v.wait_ge(expd.sem, expd.at(n + 1))
                if l >= 0:
                    ins = v.tensor_tensor(h4(K.HW[:, 2 + s, :]), key, h4(K.HW[:, s, :]), ALU.mult)
                    ins.then_inc(pkey.sem, pkey.up())
                else:
                    ins = v.tensor_tensor(h4(K.HW[:, 2 + s, :]), KK[:, 0:4, b * P:b * P + P],
                                          KK[:, 4:8, b * P:b * P + P], ALU.add)
                    ins.then_inc(pkey.sem, pkey.up())
                if l == 0 and d == 0 and b:
                    output(b - 1)
            place(len(rounds) - 1)
            output(3)

        @block.scalar
        def _(act):
            for n, (b, d, l) in enumerate(rounds):
                x = K.HW[:, n % 2, :]
                act.wait_ge(diffs.sem, diffs.at(n + 1))
                if l >= 0:
                    act.activation(x, x, ACT.Abs).then_inc(absd.sem, absd.up())
                    act.wait_ge(absd.sem, absd.last())
                    act.activation(x, x, ACT.Exp, scale=-1.0).then_inc(expd.sem, expd.up())
                else:
                    act.activation(x, x, ACT.Exp).then_inc(expd.sem, expd.up())

        @block.gpsimd
        def _(g):
            for n, (b, d, l) in enumerate(rounds):
                s = n % 2
                q = Q[:, :, b * P:b * P + P]
                g.wait_ge(expd.sem, expd.at(n + 1))
                if n >= 2:
                    g.wait_ge(scored.sem, scored.at(n - 1))
                if l >= 0:
                    dst = K.HW[:, 4 + s, :]
                else:
                    dst = K.HQ[:, 2 * (b % 2) + d, :]
                    if b >= 2:
                        g.wait_ge(summed.sem, summed.at(b - 1))
                g.tensor_tensor(h4(dst), q, h4(K.HW[:, s, :]), ALU.mult).then_inc(qk.sem, qk.up())

        @block.tensor
        def _(pe):
            def outputs(pe, b):
                pe.wait_ge(placed.sem, placed.at(15 * (b + 1)))
                if b >= 2:
                    pe.wait_ge(taken.sem, taken.at(b - 1))
                for h in range(4):
                    pairs = [(K.HA[:, b % 2, h * P:h * P + P], VA[:, b, h * P:h * P + P])]
                    for d in range(2):
                        i = orders[d].index(b)
                        if i:
                            pairs.append((K.HQ[:, 2 * (b % 2) + d, h * P:h * P + P],
                                          K.ST[:, d, i - 1, h * P:h * P + P]))
                    ins = products(pe, K.PS[:, 6 + b % 2, h * P:h * P + P], pairs)
                ins.then_inc(summed.sem, summed.up())

            for n, (b, d, l) in enumerate(rounds):
                s = n % 2
                pe.wait_ge(pkey.sem, pkey.at(n + 1))
                pe.wait_ge(qk.sem, qk.at(n + 1))
                if n >= 4:
                    m = sum(1 for r in rounds[:n - 3] if not (r[2] == -1 and r[1] == 0))
                    pe.wait_ge(placed.sem, placed.at(m))
                for h in range(4):
                    right = K.HW[:, 4 + s, h * P:h * P + P] if l >= 0 else Q[:, h, b * P:b * P + P]
                    ins = pe.matmul(K.PS[:, n % 4, h * P:h * P + P], K.HW[:, 2 + s, h * P:h * P + P], right,
                                    start=True, stop=True)
                ins.then_inc(scored.sem, scored.up())
                if l == 0 and d == 0 and b:
                    outputs(pe, b - 1)
            outputs(pe, 3)

    heads = lambda t: K.OUTB[:, t, :].rearrange("p (h w) -> p h w", h=4)
    normalise(K, (0, 1, 2, 3), P, heads, heads, groups=4)
    with K.phase("output gate") as block:
        @block.vector
        def _(v):
            v.tensor_tensor(K.OUTB[:, :, :], K.OUTB[:, :, :], GA[:, :, :], ALU.mult)
    turned_output(K, (0, 1, 2, 3), 4, lambda t, k: K.OUTB[:, t, k * P:k * P + P],
                  lambda k: K.col("hgrn_onorm", 1), lambda k: YT[:, k, :])


def window_attention(K, A, HT, YT):
    VA, QT, KD = K.VB, K.FM, K.BIG
    row = lambda r: K.LF[:, r:r + 2, :].rearrange("p a n -> p (a n)")

    def product(pe, w, bank, t):
        return products(pe, bank[:, 0:CHUNK_COLS], [(HT[:, k, t * P:t * P + P], w[:, k, :]) for k in range(KT)])

    def drain_q(eng, bank, c, o):
        return copy(K, eng, row(4 + 2 * o)[:, c * 256:c * 256 + 256], bank[:, 0:CHUNK_COLS])

    def drain_kv(eng, bank, c, t):
        if c == 1:
            return copy(K, eng, VA[:, t, 0:256], bank[:, 0:256])
        return copy(K, eng, K.LF[:, t, :].rearrange("p (g r w) -> p g r w", g=4, r=2),
                    bank[:, 0:256].rearrange("p (g r w) -> p g r w", g=4, r=1).to_broadcast([P, 4, 2, 64]))

    project(K, "latents' q", 4, 2, lambda pe, w, bank, c, o: product(pe, w, bank, o + 2), drain_q,
            engine=lambda c, o: "va"[o % 2])
    project(K, "k, v", 2, 4, lambda pe, w, bank, c, o: product(pe, w, bank, o), drain_kv,
            engine=lambda c, o: "va"[o % 2])
    axial(K, LAT, lambda t: row(2 * t), 16)
    axial(K, LAT, lambda t: K.LF[:, t, :], 8)
    turn(K, LAT, 8, lambda t, k: row(2 * t)[:, k * P:k * P + P],
         lambda eng, bank, k: copy(K, eng, QT[:, k, 0:256], bank[:, 0:256]))
    turn(K, (0, 1, 2, 3), 4, lambda t, g: K.LF[:, t, g * P:g * P + P],
         lambda eng, bank, g: copy(K, eng, KD[:, g, :], bank))
    units = []
    for t in range(2):
        for h in range(16):
            a, g = 64 * (h % 2), h // 4
            units.append(dict(
                nk=512, scale=64 ** -0.5, mask=K.BAND[:, t, :], sink=K.SINK[:, h:h + 1],
                scores=[[(QT[a:a + 64, h // 2, t * P:t * P + P], KD[a:a + 64, g, :])]],
                values=lambda i, g=g: VA[:, i, g * 64:g * 64 + 64],
                out=lambda bank, h=h: bank[:, (h % 8) * 64:(h % 8) * 64 + 64]))
    attention(K, units, 8, lambda v, bank, i: v.tensor_copy(K.BIG[:, 4 + i, :], bank))
    turn(K, LAT, 8, lambda t, k: K.BIG[:, 4 + 2 * (t - 2) + k // 4, (k % 4) * P:(k % 4) * P + P],
         lambda eng, bank, k: copy(K, eng, YT[:, k, 256:512], bank[:, 0:256]))


def latent_attention(K, A, HT, YT):
    own = K.counted("vector_step")
    low = lambda t: K.BIG[:, t - 2, :]
    wide = lambda r: K.LF[:, r:r + 2, :].rearrange("p a n -> p (a n)")
    qrow = lambda t: wide(2 * (t - 2))[:, 0:768]
    kvrow = lambda t: wide(4 + 2 * (t - 2))
    krow = lambda t: K.BIG[:, 2 + 2 * (t - 2):4 + 2 * (t - 2), :].rearrange("p a n -> p (a n)")[:, 0:768]
    h4 = lambda a: a.rearrange("p (h w) -> p h w", h=4)

    def product(pe, w, bank, c, o):
        if c < 2:
            n, t = w.shape[2], LAT[o]
            return products(pe, bank[:, 0:n], [(HT[:, k, t * P:t * P + P], w[:, k, :]) for k in range(KT)])
        return products(pe, bank[:, 0:256], [(w[:, k, o * P:o * P + P], HT[:, k, 256:512]) for k in range(KT)])

    def drain(eng, bank, c, o):
        if c == 0:
            return copy(K, eng, low(LAT[o])[:, 0:256], bank[:, 0:256])
        if c == 1:
            return copy(K, eng, low(LAT[o])[:, 256:448], bank[:, 0:192])
        if c < 4:
            return copy(K, eng, K.FM[:, 2 * (c - 2) + o, 3:259], bank[:, 0:256])
        return copy(K, eng, K.FM[:, 2 * (c - 2) + o, 0:256], bank[:, 0:256])

    project(K, "second block's projections", 6, 2, product, drain, engine=lambda c, o: "va"[o % 2])
    for a, b in ((0, 256), (256, 384)):
        part = lambda t, a=a, b=b: low(t)[:, a:b].rearrange("p (o w) -> p o w", o=1)
        normalise(K, LAT, b - a, part, part)
    turned_output(K, LAT, 3, lambda t, k: low(t)[:, k * P:k * P + P],
                  lambda k: K.col("q_a", 1, k) if k < 2 else K.col("kv_a", 1), lambda k: K.VB[:, k, 0:256])
    project(K, "q", 1, 4,
            lambda pe, w, bank, c, o: products(pe, bank[:, 0:384], [
                (K.VB[:, k, (o // 2) * P:(o // 2) * P + P], w[:, k, (o % 2) * 384:(o % 2) * 384 + 384])
                for k in range(2)]),
            lambda eng, bank, c, o: copy(K, eng, qrow(LAT[o // 2])[:, (o % 2) * 384:(o % 2) * 384 + 384],
                                         bank[:, 0:384]), engine=lambda c, o: "va"[o % 2])
    project(K, "k, v", 1, 4,
            lambda pe, w, bank, c, o: products(pe, bank, [
                (K.VB[:, 2, (o // 2) * P:(o // 2) * P + P], w[:, 0, (o % 2) * 512:(o % 2) * 512 + 512])]),
            lambda eng, bank, c, o: copy(K, eng, kvrow(LAT[o // 2])[:, (o % 2) * 512:(o % 2) * 512 + 512], bank),
            engine=lambda c, o: "va"[o % 2])
    rsum, rooted = K.counted("ranges_ready"), K.counted("roots")
    with K.phase("assemble keys and values; sines of the positions") as block:
        @block.vector
        def _(v):
            for t in LAT:
                kv = kvrow(t).rearrange("p (h w) -> p h w", h=4)
                v.tensor_copy(h4(K.VB[:, t - 2, :]), kv[:, :, P:2 * P])
                v.tensor_copy(h4(krow(t))[:, :, 0:P], kv[:, :, 0:P])
                v.tensor_copy(h4(krow(t))[:, :, P:P + 64],
                              low(t)[:, 384:448].rearrange("p (o w) -> p o w", o=1).to_broadcast([P, 4, 64]))
            v.tensor_copy(K.POSF[:, :], K.POSI[:, :]).then_inc(own.sem, own.up())
            v.wait_ge(own.sem, own.last())
            for t in range(2):
                ins = v.tensor_scalar(K.ANG[:, t, 1, :], K.INV[:, :], K.POSF[:, t:t + 1], None, ALU.mult)
                ins.then_inc(own.sem, own.up())
                v.wait_ge(own.sem, own.last())
            v.tensor_copy(K.ANG[:, :, 0, :], K.ANG[:, :, 1, :]).then_inc(own.sem, own.up())
            v.wait_ge(own.sem, own.last())
            ins = v.tensor_scalar(K.TURNS[:, :, 1, :], K.ANG[:, :, 1, :], 1.0 / TWO_PI, None, ALU.mult)
            ins.then_inc(own.sem, own.up())
            v.wait_ge(own.sem, own.last())
            ins = v.tensor_scalar(K.TURNS[:, :, 0, :], K.ANG[:, :, 0, :], 1.0 / TWO_PI, 0.25, ALU.mult, ALU.add)
            ins.then_inc(own.sem, own.up())
            v.wait_ge(own.sem, own.last())
            ins = v.tensor_scalar(K.TURNS[:, :, :, :], K.TURNS[:, :, :, :], 12582912.0, None, ALU.add)
            ins.then_inc(own.sem, own.up())
            v.wait_ge(own.sem, own.last())
            ins = v.tensor_scalar(K.TURNS[:, :, :, :], K.TURNS[:, :, :, :], 12582912.0, None, ALU.subtract)
            ins.then_inc(own.sem, own.up())
            v.wait_ge(own.sem, own.last())
            for part in (6.28125, 0.0019350051879882812, 3.0199159819567e-07):
                ins = v.scalar_tensor_tensor(K.ANG[:, :, :, :], K.TURNS[:, :, :, :], -part,
                                             K.ANG[:, :, :, :], ALU.mult, ALU.add)
                ins.then_inc(own.sem, own.up())
                v.wait_ge(own.sem, own.last())
            ins = v.tensor_scalar(K.ANG[:, :, 0, :], K.ANG[:, :, 0, :], math.pi / 2, None, ALU.add)
            ins.then_inc(own.sem, own.up())
            v.wait_ge(own.sem, own.last())
            ins = v.tensor_scalar(K.ANG[:, :, :, :], K.ANG[:, :, :, :], 3.1415925, -3.1415925, ALU.min, ALU.max)
            ins.then_inc(rsum.sem, rsum.up())
            v.wait_ge(rooted.sem, rooted.at(1))
            for j in range(2):
                v.tensor_copy(K.TRIG[:, :, 0, j * 32:j * 32 + 32], K.ANG[:, :, 0, :])
                v.tensor_scalar(K.TRIG[:, :, 1, j * 32:j * 32 + 32], K.ANG[:, :, 1, :], 2.0 * j - 1.0, None, ALU.mult)

        @block.scalar
        def _(act):
            act.wait_ge(rsum.sem, rsum.at(1))
            act.activation(K.ANG[:, :, :, :], K.ANG[:, :, :, :], ACT.Sin).then_inc(rooted.sem, rooted.up())

    for i, row in enumerate((qrow, krow)):
        heads = lambda t, row=row: h4(row(t))
        normalise(K, LAT, 192, heads, heads, groups=4)
        with K.phase("gain") as block:
            @block.vector
            def _(v):
                g = K.QKN[:, i:i + 1, :].to_broadcast([P, 4, 192])
                for t in LAT:
                    v.tensor_tensor(heads(t), heads(t), g, ALU.mult)
        rotate(K, LAT, lambda t: heads(t)[:, :, P:P + 64],
               lambda t: (K.TRIG[:, t - 2, 0, :], K.TRIG[:, t - 2, 1, :]), K.SQ)
        turn(K, LAT, 8, lambda t, k: heads(t)[:, k, 0:P] if k < 4 else heads(t)[:, k - 4, P:P + 64],
             lambda eng, bank, k, i=i: copy(K, eng, HT[0:P if k < 4 else 64, k, i * 256:i * 256 + 256],
                                            bank[0:P if k < 4 else 64, 0:256]))
    units = []
    for t in range(2):
        nk = (t + 1) * P
        for h in range(4):
            q = slice(t * P, t * P + P)
            units.append(dict(
                nk=nk, scale=192 ** -0.5, mask=K.CAUSAL[:, 256 - nk:256] if t else K.CAUSAL[:, 128:256], sink=None,
                scores=[[(HT[:, h, q], HT[:, h, 256:256 + nk]), (HT[0:64, 4 + h, q], HT[0:64, 4 + h, 256:256 + nk])]],
                values=lambda i, h=h: K.VB[:, i, h * P:h * P + P],
                out=lambda bank, h=h: bank[:, h * P:h * P + P]))
    attention(K, units, 4, lambda v, bank, i: v.tensor_copy(K.BIG[:, i, :], bank))
    whole = lambda t: K.BIG[:, t - 2:t - 1, :]
    normalise(K, LAT, 512, whole, whole)
    turned_output(K, LAT, 4, lambda t, k: K.BIG[:, t - 2, k * P:k * P + P], lambda k: K.col("attn_out", 1, k),
                  lambda k: YT[:, k, 256:512])


def lru(K, A, YT):
    own, soft, act_own = K.counted("vector_step"), K.counted("softplus_ready"), K.counted("scalar_step")
    XC = K.LF[:, 0:4, 0:256]
    with K.phase("convolution") as block:
        @block.vector
        def _(v):
            v.memset(K.FM[:, 0:4, 0:3], 0.0).then_inc(own.sem, own.up())
            v.wait_ge(own.sem, own.last())
            for j in range(4):
                ins = v.tensor_scalar(XC[:, j, :], K.FM[:, j, 0:256], K.col("conv_w", 1, j),
                                      K.col("conv_b", 1, j), ALU.mult, ALU.add)
                ins.then_inc(own.sem, own.up())
                v.wait_ge(own.sem, own.last())
                for i in range(1, 4):
                    ins = v.scalar_tensor_tensor(XC[:, j, :], K.FM[:, j, i:i + 256],
                                                 K.col("conv_w", 1, 4 * i + j), XC[:, j, :],
                                                 ALU.mult, ALU.add)
                    ins.then_inc(own.sem, own.up())
                    v.wait_ge(own.sem, own.last())
            ins = v.tensor_scalar(K.SPL[:, 0:4], K.col("lambda", 4), -1.0, 0.0, ALU.mult, ALU.max)
            ins.then_inc(own.sem, own.up())
            v.wait_ge(own.sem, own.last())
            v.tensor_scalar(K.SPL[:, 4:8], K.col("lambda", 4), 0.0, None, ALU.max).then_inc(own.sem, own.up())
            v.wait_ge(own.sem, own.last())
            v.tensor_tensor(K.SPL[:, 4:8], K.SPL[:, 4:8], K.SPL[:, 0:4], ALU.add).then_inc(own.sem, own.up())
            v.wait_ge(own.sem, own.last())
            v.tensor_copy(K.SPL[:, 8:12], K.SPL[:, 4:8]).then_inc(soft.sem, soft.up())
            v.wait_ge(soft.sem, soft.at(2))
            v.tensor_tensor(K.SPL[:, 0:4], K.SPL[:, 0:4], K.SPL[:, 8:12], ALU.add).then_inc(own.sem, own.up())
            v.wait_ge(own.sem, own.last())
            v.tensor_scalar(K.SPL[:, 0:4], K.SPL[:, 0:4], -8.0, None, ALU.mult)
            v.tensor_copy(K.POSG[:, 0, :], K.POSR[:, :]).then_inc(own.sem, own.up())
            v.wait_ge(own.sem, own.last())
            v.tensor_scalar(K.POSG[:, 1, :], K.POSG[:, 0, :], 0.0, None, ALU.is_equal).then_inc(own.sem, own.up())
            v.wait_ge(own.sem, own.last())
            v.tensor_scalar(K.POSG[:, 0, :], K.POSG[:, 1, :], -1.0, 1.0, ALU.mult, ALU.add)

        @block.scalar
        def _(act):
            act.wait_ge(soft.sem, soft.at(1))
            act.activation(K.SPL[:, 8:12], K.SPL[:, 8:12], ACT.Exp, scale=-1.0).then_inc(act_own.sem, act_own.up())
            act.wait_ge(act_own.sem, act_own.last())
            act.activation(K.SPL[:, 8:12], K.SPL[:, 8:12], ACT.Ln, bias=1.0).then_inc(soft.sem, soft.up())

    project(K, "LRU gates", 2, 4,
            lambda pe, w, bank, c, o: products(pe, bank[:, 0:256], [(w[:, o, :], XC[:, o, :])]),
            lambda eng, bank, c, o: eng.activation(K.LF[:, 4 + o, 256 * c:256 * c + 256], bank[:, 0:256], ACT.Sigmoid,
                                                   bias=K.col("lru_ba" if c == 0 else "lru_bx", 1, o)),
            engine=lambda c, o: "a")
    A_, M_, B_, H_ = (K.BIG[:, 2 * i:2 * i + 2, :].rearrange("p a (b n) -> p (a b) n", b=2) for i in range(4))
    la, ea, sa, ga, gb = (K.counted(n) for n in ("log_decay", "decay", "multiplier", "cube_ready", "gelu_ready"))
    G = K.FM[:, 4:8, 0:256]
    keep = K.POSG[:, 0:1, :].to_broadcast([P, 4, 256])
    reset = K.POSG[:, 1:2, :].to_broadcast([P, 4, 256])
    with K.phase("LRU") as block:
        @block.vector
        def _(v):
            for j in range(4):
                ins = v.tensor_scalar(A_[:, j, :], K.LF[:, 4 + j, 0:256], K.SPL[:, j:j + 1], None, ALU.mult)
            ins.then_inc(la.sem, la.up())
            v.tensor_tensor(H_, G, G, ALU.mult).then_inc(own.sem, own.up())
            v.wait_ge(own.sem, own.last())
            v.tensor_scalar(H_, H_, 0.044715, 1.0, ALU.mult, ALU.add).then_inc(own.sem, own.up())
            v.wait_ge(own.sem, own.last())
            v.tensor_tensor(H_, H_, G, ALU.mult).then_inc(ga.sem, ga.up())
            v.wait_ge(ea.sem, ea.at(2))
            v.tensor_tensor(A_, A_, keep, ALU.mult).then_inc(own.sem, own.up())
            v.wait_ge(own.sem, own.last())
            v.tensor_scalar(M_, M_, -1.0, 1.0, ALU.mult, ALU.add).then_inc(own.sem, own.up())
            v.wait_ge(own.sem, own.last())
            v.tensor_scalar(M_, M_, 2.0 ** -100, None, ALU.max).then_inc(sa.sem, sa.up())
            v.tensor_tensor(B_, K.LF[:, 4:8, 256:512], XC, ALU.mult).then_inc(own.sem, own.up())
            v.wait_ge(own.sem, own.last())
            v.wait_ge(sa.sem, sa.at(2))
            v.tensor_tensor(M_, M_, keep, ALU.mult).then_inc(own.sem, own.up())
            v.wait_ge(own.sem, own.last())
            v.tensor_tensor(M_, M_, reset, ALU.add).then_inc(own.sem, own.up())
            v.wait_ge(own.sem, own.last())
            v.tensor_tensor(B_, B_, M_, ALU.mult).then_inc(own.sem, own.up())
            v.wait_ge(own.sem, own.last())
            for j in range(4):
                ins = v.tensor_tensor_scan(B_[:, j, :], A_[:, j, :], B_[:, j, :], 0.0, ALU.mult, ALU.add)
                ins.then_inc(own.sem, own.up())
                v.wait_ge(own.sem, own.last())
            v.wait_ge(gb.sem, gb.at(1))
            v.tensor_tensor(H_, H_, G, ALU.mult).then_inc(own.sem, own.up())
            v.wait_ge(own.sem, own.last())
            v.tensor_tensor(B_, B_, H_, ALU.mult).then_inc(own.sem, own.up())
            v.wait_ge(own.sem, own.last())
            v.tensor_tensor(H_, B_, B_, ALU.mult)

        @block.scalar
        def _(act):
            act.wait_ge(la.sem, la.at(1))
            act.activation(M_, A_, ACT.Exp, scale=2.0).then_inc(ea.sem, ea.up())
            act.activation(A_, A_, ACT.Exp).then_inc(ea.sem, ea.up())
            act.wait_ge(ga.sem, ga.at(1))
            act.activation(H_, H_, ACT.Sigmoid, scale=2.0 * math.sqrt(2.0 / math.pi)).then_inc(gb.sem, gb.up())
            act.wait_ge(sa.sem, sa.at(1))
            act.activation(M_, M_, ACT.Sqrt).then_inc(sa.sem, sa.up())

    sums, root = K.counted("square_sums"), K.counted("roots")
    R = K.SQ[:, 0:256]
    with K.phase("LRU norm") as block:
        @block.tensor
        def _(pe):
            ins = products(pe, K.PS[:, 0, 0:256], [(K.ONES[:, :], H_[:, j, :]) for j in range(4)])
            ins.then_inc(sums.sem, sums.up())

        @block.vector
        def _(v):
            v.wait_ge(sums.sem, sums.at(1))
            v.tensor_scalar(R, K.PS[:, 0, 0:256], 1.0 / 512, EPS, ALU.mult, ALU.add).then_inc(root.sem, root.up())
            v.wait_ge(root.sem, root.at(2))
            v.reciprocal(R, R).then_inc(own.sem, own.up())
            v.wait_ge(own.sem, own.last())
            for j in range(4):
                v.scalar_tensor_tensor(YT[:, 4 + j, 256:512], B_[:, j, :], K.col("lru_out", 1, j), R,
                                       ALU.mult, ALU.mult)

        @block.scalar
        def _(act):
            act.wait_ge(root.sem, root.at(1))
            act.activation(R, R, ACT.Sqrt).then_inc(root.sem, root.up())


def ranks_below(K, v, own, s, n, groups, out):
    w = groups * n * n
    gt = K.SQ[:, 0:w].rearrange("p (g i j) -> p g i j", g=groups, i=n)
    eq = K.SQ[:, w:2 * w].rearrange("p (g i j) -> p g i j", g=groups, i=n)
    si = s.rearrange("p g (i o) -> p g i o", o=1).to_broadcast([P, groups, n, n])
    sj = s.rearrange("p g (o j) -> p g o j", o=1).to_broadcast([P, groups, n, n])
    before = K.BEFORE[:, 0:n * n] if n == 4 else K.BEFORE[:, 16:16 + n * n]
    bf = before.rearrange("p (o i j) -> p o i j", o=1, i=n).to_broadcast([P, groups, n, n])
    v.tensor_tensor(gt, sj, si, ALU.is_gt)
    v.tensor_tensor(eq, sj, si, ALU.is_equal).then_inc(own.sem, own.up())
    v.wait_ge(own.sem, own.last())
    v.tensor_tensor(eq, eq, bf, ALU.mult).then_inc(own.sem, own.up())
    v.wait_ge(own.sem, own.last())
    v.tensor_tensor(gt, gt, eq, ALU.add).then_inc(own.sem, own.up())
    v.wait_ge(own.sem, own.last())
    v.tensor_reduce(out, gt, AX.X, ALU.add).then_inc(own.sem, own.up())
    v.wait_ge(own.sem, own.last())


def route_first(K, NT):
    own, exps = K.counted("vector_step"), K.counted("exponentials_ready")
    with K.phase("route") as block:
        @block.scalar
        def _(act):
            for t in range(NT):
                ins = act.activation(K.RW[:, t, 0:16], K.PS[:, 0, t * 16:t * 16 + 16], ACT.Sigmoid)
            ins.then_inc(exps.sem, exps.up())

        @block.vector
        def _(v):
            v.wait_ge(exps.sem, exps.at(1))
            for t in range(NT):
                aff = K.RW[:, t, 0:16]
                sel, top, gs, gr = K.RT[:, 0:16], K.RT[:, 32:48], K.RT[:, 64:68], K.RT[:, 72:76]
                g4 = lambda a: a.rearrange("p (g e) -> p g e", g=4)
                v.tensor_tensor(sel, aff, K.RB[:, 0:16], ALU.add).then_inc(own.sem, own.up())
                v.wait_ge(own.sem, own.last())
                ranks_below(K, v, own, g4(sel), 4, 4, g4(top))
                v.tensor_scalar(top, top, 2.0, None, ALU.is_lt).then_inc(own.sem, own.up())
                v.wait_ge(own.sem, own.last())
                v.tensor_tensor(sel, sel, top, ALU.mult).then_inc(own.sem, own.up())
                v.wait_ge(own.sem, own.last())
                v.tensor_reduce(gs, g4(sel), AX.X, ALU.add).then_inc(own.sem, own.up())
                v.wait_ge(own.sem, own.last())
                ranks_below(K, v, own, gs.rearrange("p (o e) -> p o e", o=1), 4, 1,
                            gr.rearrange("p (o e) -> p o e", o=1))
                v.tensor_scalar(gr, gr, 1.0, None, ALU.is_lt).then_inc(own.sem, own.up())
                v.wait_ge(own.sem, own.last())
                ins = v.tensor_tensor(g4(K.RM[:, t, 0:16]), g4(top),
                                      gr.rearrange("p (g o) -> p g o", o=1).to_broadcast([P, 4, 4]), ALU.mult)
                ins.then_inc(own.sem, own.up())
                v.wait_ge(own.sem, own.last())
                v.tensor_tensor(aff, aff, K.RM[:, t, 0:16], ALU.mult).then_inc(own.sem, own.up())
                v.wait_ge(own.sem, own.last())
                v.tensor_reduce(gs[:, 0:1], aff, AX.X, ALU.add).then_inc(own.sem, own.up())
                v.wait_ge(own.sem, own.last())
                v.reciprocal(gs[:, 0:1], gs[:, 0:1]).then_inc(own.sem, own.up())
                v.wait_ge(own.sem, own.last())
                v.tensor_scalar(aff, aff, gs[:, 0:1], None, ALU.mult).then_inc(own.sem, own.up())
                v.wait_ge(own.sem, own.last())


def route_second(K, NT):
    own, less, exps = K.counted("vector_step"), K.counted("logits_ready"), K.counted("exponentials_ready")
    with K.phase("route") as block:
        @block.scalar
        def _(act):
            for t in range(NT):
                act.wait_ge(less.sem, less.at(t + 1))
                act.activation(K.RT[:, 0:36], K.RT[:, 0:36], ACT.Exp).then_inc(exps.sem, exps.up())

        @block.vector
        def _(v):
            for t in range(NT):
                x, gl, el = K.RT[:, 0:36], K.RT[:, 0:4], K.RT[:, 4:36]
                mx, gr, top, gp = K.RT[:, 40:45], K.RT[:, 48:52], K.RT[:, 64:96], K.RT[:, 56:57]
                g8 = lambda a: a.rearrange("p (g e) -> p g e", g=4)
                ins = v.tensor_tensor(x, K.PS[:, 0, t * 36:t * 36 + 36], K.RB[:, 16:52], ALU.add)
                ins.then_inc(own.sem, own.up())
                v.wait_ge(own.sem, own.last())
                v.tensor_reduce(mx[:, 0:1], gl, AX.X, ALU.max)
                v.tensor_reduce(mx[:, 1:5], g8(el), AX.X, ALU.max).then_inc(own.sem, own.up())
                v.wait_ge(own.sem, own.last())
                v.tensor_scalar(gl, gl, mx[:, 0:1], None, ALU.subtract)
                ins = v.tensor_tensor(g8(el), g8(el), mx[:, 1:5].rearrange("p (g o) -> p g o", o=1)
                                      .to_broadcast([P, 4, 8]), ALU.subtract)
                ins.then_inc(less.sem, less.up())
                v.wait_ge(exps.sem, exps.at(t + 1))
                v.tensor_reduce(mx[:, 0:1], gl, AX.X, ALU.add)
                v.tensor_reduce(mx[:, 1:5], g8(el), AX.X, ALU.add).then_inc(own.sem, own.up())
                v.wait_ge(own.sem, own.last())
                v.reciprocal(mx, mx).then_inc(own.sem, own.up())
                v.wait_ge(own.sem, own.last())
                v.tensor_scalar(gl, gl, mx[:, 0:1], None, ALU.mult)
                ins = v.tensor_tensor(g8(el), g8(el), mx[:, 1:5].rearrange("p (g o) -> p g o", o=1)
                                      .to_broadcast([P, 4, 8]), ALU.mult)
                ins.then_inc(own.sem, own.up())
                v.wait_ge(own.sem, own.last())
                v.tensor_reduce(gp, gl, AX.X, ALU.max).then_inc(own.sem, own.up())
                v.wait_ge(own.sem, own.last())
                ranks_below(K, v, own, gl.rearrange("p (o e) -> p o e", o=1), 4, 1,
                            gr.rearrange("p (o e) -> p o e", o=1))
                v.tensor_scalar(gr, gr, 1.0, None, ALU.is_lt).then_inc(own.sem, own.up())
                v.wait_ge(own.sem, own.last())
                ranks_below(K, v, own, g8(el), 8, 4, g8(top))
                v.tensor_scalar(top, top, 2.0, None, ALU.is_lt).then_inc(own.sem, own.up())
                v.wait_ge(own.sem, own.last())
                ins = v.tensor_tensor(g8(K.RM[:, t, :]), g8(top),
                                      gr.rearrange("p (g o) -> p g o", o=1).to_broadcast([P, 4, 8]), ALU.mult)
                ins.then_inc(own.sem, own.up())
                v.wait_ge(own.sem, own.last())
                w = K.RW[:, t, :]
                v.tensor_tensor(w, el, K.RM[:, t, :], ALU.mult).then_inc(own.sem, own.up())
                v.wait_ge(own.sem, own.last())
                v.tensor_reduce(mx[:, 0:1], w, AX.X, ALU.add).then_inc(own.sem, own.up())
                v.wait_ge(own.sem, own.last())
                v.reciprocal(mx[:, 0:1], mx[:, 0:1]).then_inc(own.sem, own.up())
                v.wait_ge(own.sem, own.last())
                v.tensor_scalar(w, w, mx[:, 0:1], gp, ALU.mult, ALU.mult).then_inc(own.sem, own.up())
                v.wait_ge(own.sem, own.last())


def single_experts(K, NT, E, F, C, rows, H2, ACC):
    FT = F // P
    XG = rows(16, 4).rearrange("p (s a) n -> p s (a n)", a=2)
    HID = rows(20, 4).rearrange("p (s a) n -> p s (a n)", a=2)
    GS = rows(24, 2).rearrange("p a n -> p (a n)")
    Y = rows(26, 2).rearrange("p a n -> p (a n)")
    SEL, SELW, SELT = rows(28, 2), rows(30, 2), rows(40, 2)
    NG, ND = F // CHUNK_COLS, (4 if F == D else 1)
    CH = 2 * NG + ND
    uses = []
    spread_uses = lambda e: [("selt", e, 0), ("gather", e, 0), ("gather", e, 1)]
    uses += spread_uses(0)
    for e in range(E):
        if e:
            uses += [("scatter", e - 1, i) for i in range(2 * NT)]
        if e + 1 < E:
            uses += spread_uses(e + 1)
    uses += [("scatter", E - 1, i) for i in range(2 * NT)]
    number = {u: i for i, u in enumerate(uses)}
    util, released = K.counted("bank_filled"), K.released
    drained = [K.counted("bank_6_drained"), K.counted("bank_7_drained")]
    selected, silus, hidden, copied = (K.counted(n) for n in (
        "selections_ready", "silu_ready", "hidden_ready", "expert_outputs_copied"))
    per_bank = 512 // C
    spans = [(b, b * per_bank, min(FT, (b + 1) * per_bank)) for b in range(-(-FT // per_bank))]
    with K.phase("experts") as block:
        @block.sync
        def _(sp):
            K.feed(sp, CH * E)

        @block.tensor
        def _(pe):
            def bank_for(use):
                u = number[use]
                if u >= 2:
                    pe.wait_ge(drained[u % 2].sem, drained[u % 2].at(u // 2))
                return K.PS[:, 6 + u % 2, :]

            def gather(e):
                pe.wait_ge(selected.sem, selected.at(e + 1))
                bank = bank_for(("selt", e, 0))
                for t in range(NT):
                    ins = pe.transpose(bank[0:C, t * P:t * P + P], SELW[:, e % 2, t * P:t * P + C], K.IDENT[:, :])
                ins.then_inc(util.sem, util.up())
                for half in range(2):
                    bank = bank_for(("gather", e, half))
                    for k in range(4):
                        ins = products(pe, bank[:, k * C:k * C + C],
                                       [(H2[:, t, (4 * half + k) * P:(4 * half + k + 1) * P],
                                         SEL[:, e % 2, t * P:t * P + C]) for t in range(NT)])
                    ins.then_inc(util.sem, util.up())

            def scatter(e):
                pe.wait_ge(copied.sem, copied.at(e + 1))
                for t in range(NT):
                    for half in range(2):
                        bank = bank_for(("scatter", e, 2 * t + half))
                        ins = pe.matmul(bank, SELT[0:C, e % 2, t * P:t * P + P],
                                        Y[0:C, half * 512:half * 512 + 512], start=True, stop=True)
                        ins.then_inc(util.sem, util.up())

            def up_or_gate(e, first_bank):
                for c in range(NG):
                    w = K.take(pe)
                    for f in range(2):
                        j = 2 * c + f
                        out = K.PS[:, first_bank + j // per_bank, (j % per_bank) * C:(j % per_bank + 1) * C]
                        ins = products(pe, out, [(w[:, k, f * P:f * P + P], XG[:, e % 2, k * C:k * C + C])
                                                 for k in range(KT)])
                    ins.then_inc(released.sem, released.up())

            gather(0)
            for e in range(E):
                pe.wait_ge(drained[number[("gather", e, 1)] % 2].sem, drained[number[("gather", e, 1)] % 2].at(number[("gather", e, 1)] // 2 + 1))
                pe.wait_ge(drained[number[("gather", e, 0)] % 2].sem, drained[number[("gather", e, 0)] % 2].at(number[("gather", e, 0)] // 2 + 1))
                if e:
                    pe.wait_ge(silus.sem, silus.at(e))
                up_or_gate(e, 0)
                if e:
                    scatter(e - 1)
                    pe.wait_ge(hidden.sem, hidden.at(e))
                up_or_gate(e, 2)
                if e + 1 < E:
                    gather(e + 1)
                pe.wait_ge(hidden.sem, hidden.at(e + 1))
                if e:
                    pe.wait_ge(copied.sem, copied.at(e))
                for c in range(ND):
                    w = K.take(pe)
                    if F == D:
                        out = K.PS[0:C, 4 + c // 2, (c % 2) * 256:(c % 2) * 256 + 256]
                        ins = products(pe, out, [(HID[:, e % 2, k * C:k * C + C], w[:, k, :]) for k in range(FT)])
                    else:
                        for half in range(2):
                            ins = products(pe, K.PS[0:C, 4 + half, :],
                                           [(HID[:, e % 2, k * C:k * C + C], w[:, k, half * 512:half * 512 + 512])
                                            for k in range(FT)])
                    ins.then_inc(released.sem, released.up())
            scatter(E - 1)

        @block.vector
        def _(v):
            def select(e):
                if e >= 2:
                    v.wait_ge(util.sem, util.at(number[("gather", e - 2, 1)] + 1))
                for t in range(NT):
                    v.tensor_scalar(SEL[:, e % 2, t * P:t * P + C], K.IOTA[:, 0:C], K.RP[:, t, e:e + 1], None,
                                    ALU.is_equal)
                    ins = v.tensor_scalar(SELW[:, e % 2, t * P:t * P + C], K.IOTA[:, 0:C], K.RP[:, t, e:e + 1],
                                          K.RW[:, t, e:e + 1], ALU.is_equal, ALU.mult)
                ins.then_inc(selected.sem, selected.up())

            def add(e):
                for t in range(NT):
                    for half in range(2):
                        u = number[("scatter", e, 2 * t + half)]
                        v.wait_ge(util.sem, util.at(u + 1))
                        a = ACC[:, t, half * 512:half * 512 + 512]
                        ins = v.tensor_tensor(a, a, K.PS[:, 6 + u % 2, :], ALU.add)
                        ins.then_inc(drained[u % 2].sem, drained[u % 2].up())

            select(0)
            for e in range(E):
                if e + 1 < E:
                    select(e + 1)
                if e:
                    add(e - 1)
                v.wait_ge(silus.sem, silus.at(e + 1))
                v.wait_ge(released.sem, released.at(e * CH + 2 * NG))
                if e >= 2:
                    v.wait_ge(released.sem, released.at((e - 1) * CH))
                for b, f0, f1 in spans:
                    ins = v.tensor_tensor(HID[:, e % 2, f0 * C:f1 * C], GS[:, f0 * C:f1 * C],
                                          K.PS[:, 2 + b, 0:(f1 - f0) * C], ALU.mult)
                ins.then_inc(hidden.sem, hidden.up())
            add(E - 1)

        @block.scalar
        def _(act):
            def drains(e):
                u = number[("selt", e, 0)]
                act.wait_ge(util.sem, util.at(u + 1))
                ins = act.activation(SELT[0:C, e % 2, 0:NT * P], K.PS[0:C, 6 + u % 2, 0:NT * P], ACT.Copy)
                ins.then_inc(drained[u % 2].sem, drained[u % 2].up())
                for half in range(2):
                    u = number[("gather", e, half)]
                    act.wait_ge(util.sem, util.at(u + 1))
                    ins = act.activation(XG[:, e % 2, half * 4 * C:(half + 1) * 4 * C],
                                         K.PS[:, 6 + u % 2, 0:4 * C], ACT.Copy)
                    ins.then_inc(drained[u % 2].sem, drained[u % 2].up())

            drains(0)
            for e in range(E):
                act.wait_ge(released.sem, released.at(e * CH + NG))
                if e:
                    act.wait_ge(hidden.sem, hidden.at(e))
                for b, f0, f1 in spans:
                    ins = act.activation(GS[:, f0 * C:f1 * C], K.PS[:, b, 0:(f1 - f0) * C], ACT.Silu)
                ins.then_inc(silus.sem, silus.up())
                if e + 1 < E:
                    drains(e + 1)
                act.wait_ge(released.sem, released.at((e + 1) * CH))
                for half in range(2):
                    ins = act.activation(Y[0:C, half * 512:half * 512 + 512], K.PS[0:C, 4 + half, :], ACT.Copy)
                ins.then_inc(copied.sem, copied.up())


def pair_order(E, F):
    NG, ND = F // CHUNK_COLS, (4 if F == D else 1)
    part = lambda m, q, n: [(m, 2 * q + i, c) for c in range(n) for i in range(2)]
    order = []
    for q in range(E // 2):
        order += part("gate", q, NG)
        if q:
            order += part("down", q - 1, ND)
        order += part("up", q, NG)
    return order + part("down", E // 2 - 1, ND)


def paired_experts(K, NT, E, F, C, rows, H2, ACC):
    assert 2 * C == P
    Q, FT = E // 2, F // P
    NG, ND = F // CHUNK_COLS, (4 if F == D else 1)
    flat = lambda a: a.rearrange("p a n -> p (a n)")
    XG = rows(16, 4).rearrange("p (s a) n -> p s (a n)", a=2)
    HID, HIDT, GS, Y = (flat(rows(a, 2)) for a in (20, 22, 24, 26))
    SEL, SELW, SELT = rows(28, 2), rows(30, 2), rows(40, 2)
    order = pair_order(E, F)
    place = {chunk: i + 1 for i, chunk in enumerate(order)}
    done = lambda m, q: place[(m, 2 * q + 1, (ND if m == "down" else NG) - 1)]
    turns = -(-FT // 4)
    uses = [("selt", 0, 0), ("gather", 0, 0), ("gather", 0, 1)]
    for q in range(Q):
        if q:
            uses += [("scatter", q - 1, i) for i in range(2 * NT)]
        if q + 1 < Q:
            uses += [("selt", q + 1, 0), ("gather", q + 1, 0), ("gather", q + 1, 1)]
        uses += [("turn", q, i) for i in range(turns)]
    uses += [("scatter", Q - 1, i) for i in range(2 * NT)]
    number = {u: i for i, u in enumerate(uses)}
    util, released = K.counted("bank_filled"), K.released
    drained = [K.counted("bank_6_drained"), K.counted("bank_7_drained")]
    selected, silus, hidden, copied = (K.counted(n) for n in (
        "selections_ready", "silu_ready", "hidden_ready", "expert_outputs_copied"))
    width = min(F, 512)
    with K.phase("paired experts") as block:
        @block.sync
        def _(sp):
            K.feed(sp, len(order))

        @block.tensor
        def _(pe):
            def bank_for(use):
                u = number[use]
                if u >= 2:
                    pe.wait_ge(drained[u % 2].sem, drained[u % 2].at(u // 2))
                return K.PS[:, 6 + u % 2, :]

            def read(use):
                u = number[use]
                pe.wait_ge(drained[u % 2].sem, drained[u % 2].at(u // 2 + 1))

            def gather(q):
                pe.wait_ge(selected.sem, selected.at(q + 1))
                bank = bank_for(("selt", q, 0))
                for t in range(NT):
                    ins = pe.transpose(bank[:, t * P:t * P + P], SELW[:, q % 2, t * P:t * P + P], K.IDENT[:, :])
                ins.then_inc(util.sem, util.up())
                for half in range(2):
                    bank = bank_for(("gather", q, half))
                    for k in range(4):
                        ins = products(pe, bank[:, k * P:k * P + P],
                                       [(H2[:, t, (4 * half + k) * P:(4 * half + k + 1) * P],
                                         SEL[:, q % 2, t * P:t * P + P]) for t in range(NT)])
                    ins.then_inc(util.sem, util.up())

            def scatter(q):
                pe.wait_ge(copied.sem, copied.at(q + 1))
                for t in range(NT):
                    for half in range(2):
                        bank = bank_for(("scatter", q, 2 * t + half))
                        pe.matmul(bank, SELT[:, q % 2, t * P:t * P + P], Y[:, half * 512:half * 512 + 512],
                                  start=True, stop=True).then_inc(util.sem, util.up())

            def side_by_side(pair, out, left, right, n):
                for k in range(n):
                    for i in range(2):
                        ins = pe.matmul(out(i), left(i, k), right(pair[i], k), start=k == 0, stop=k == n - 1,
                                        skip_group_check=True)
                        if k == n - 1:
                            yield ins

            def gate_or_up(q, first_bank):
                for c in range(NG):
                    pair = [K.take(pe), K.take(pe)]
                    at = c * CHUNK_COLS
                    out = lambda i: K.PS[i * C:i * C + C, first_bank + at // 512, at % 512:at % 512 + CHUNK_COLS]
                    for ins in side_by_side(pair, out, lambda i, k: XG[:, q % 2, k * P + i * C:k * P + i * C + C],
                                            lambda w, k: w[:, k, :], KT):
                        ins.then_inc(released.sem, released.up())

            def turn_hidden(q):
                pe.wait_ge(hidden.sem, hidden.at(q + 1))
                for b in range(turns):
                    bank = bank_for(("turn", q, b))
                    for j in range(4 * b, min(FT, 4 * b + 4)):
                        ins = pe.transpose(bank[:, (j - 4 * b) * P:(j - 4 * b + 1) * P], HID[:, j * P:j * P + P],
                                           K.IDENT[:, :])
                    ins.then_inc(util.sem, util.up())

            def down(q):
                for b in range(turns):
                    read(("turn", q, b))
                if q:
                    pe.wait_ge(copied.sem, copied.at(q))
                left = lambda i, k: HIDT[:, k * P + i * C:k * P + i * C + C]
                for c in range(ND):
                    pair = [K.take(pe), K.take(pe)]
                    if F == D:
                        out = lambda i: K.PS[i * C:i * C + C, 4 + c // 2, (c % 2) * 256:(c % 2) * 256 + 256]
                        for ins in side_by_side(pair, out, left, lambda w, k: w[:, k, :], FT):
                            ins.then_inc(released.sem, released.up())
                        continue
                    for half in range(2):
                        out = lambda i: K.PS[i * C:i * C + C, 4 + half, :]
                        for ins in side_by_side(pair, out, left,
                                                lambda w, k: w[:, k, half * 512:half * 512 + 512], FT):
                            if half == 1:
                                ins.then_inc(released.sem, released.up())

            gather(0)
            for q in range(Q):
                read(("gather", q, 0))
                read(("gather", q, 1))
                if q:
                    pe.wait_ge(silus.sem, silus.at(q))
                gate_or_up(q, 0)
                if q:
                    down(q - 1)
                    pe.wait_ge(hidden.sem, hidden.at(q))
                gate_or_up(q, 2)
                if q:
                    scatter(q - 1)
                if q + 1 < Q:
                    gather(q + 1)
                turn_hidden(q)
            down(Q - 1)
            scatter(Q - 1)

        @block.vector
        def _(v):
            def select(q):
                if q >= 2:
                    v.wait_ge(util.sem, util.at(number[("gather", q - 2, 1)] + 1))
                for t in range(NT):
                    for i in range(2):
                        e, cols = 2 * q + i, slice(t * P + i * C, t * P + i * C + C)
                        v.tensor_scalar(SEL[:, q % 2, cols], K.IOTA[:, 0:C], K.RP[:, t, e:e + 1], None,
                                        ALU.is_equal)
                        ins = v.tensor_scalar(SELW[:, q % 2, cols], K.IOTA[:, 0:C], K.RP[:, t, e:e + 1],
                                              K.RW[:, t, e:e + 1], ALU.is_equal, ALU.mult)
                ins.then_inc(selected.sem, selected.up())

            def add(q):
                for t in range(NT):
                    for half in range(2):
                        u = number[("scatter", q, 2 * t + half)]
                        v.wait_ge(util.sem, util.at(u + 1))
                        a = ACC[:, t, half * 512:half * 512 + 512]
                        v.tensor_tensor(a, a, K.PS[:, 6 + u % 2, :], ALU.add
                                        ).then_inc(drained[u % 2].sem, drained[u % 2].up())

            select(0)
            for q in range(Q):
                if q + 1 < Q:
                    select(q + 1)
                v.wait_ge(silus.sem, silus.at(q + 1))
                v.wait_ge(released.sem, released.at(done("up", q)))
                if q:
                    v.wait_ge(util.sem, util.at(number[("turn", q - 1, turns - 1)] + 1))
                for b in range(F // width):
                    ins = v.tensor_tensor(HID[:, b * width:(b + 1) * width], GS[:, b * width:(b + 1) * width],
                                          K.PS[:, 2 + b, 0:width], ALU.mult)
                ins.then_inc(hidden.sem, hidden.up())
                if q:
                    add(q - 1)
                u = number[("turn", q, 0)]
                v.wait_ge(util.sem, util.at(u + 1))
                v.tensor_copy(HIDT[:, 0:width], K.PS[:, 6 + u % 2, 0:width]
                              ).then_inc(drained[u % 2].sem, drained[u % 2].up())
            add(Q - 1)

        @block.scalar
        def _(act):
            def drains(q):
                u = number[("selt", q, 0)]
                act.wait_ge(util.sem, util.at(u + 1))
                act.activation(SELT[:, q % 2, 0:NT * P], K.PS[:, 6 + u % 2, 0:NT * P], ACT.Copy
                               ).then_inc(drained[u % 2].sem, drained[u % 2].up())
                for half in range(2):
                    u = number[("gather", q, half)]
                    act.wait_ge(util.sem, util.at(u + 1))
                    act.activation(XG[:, q % 2, half * 512:half * 512 + 512], K.PS[:, 6 + u % 2, :], ACT.Copy
                                   ).then_inc(drained[u % 2].sem, drained[u % 2].up())

            def outputs(q):
                act.wait_ge(released.sem, released.at(done("down", q)))
                if q:
                    act.wait_ge(util.sem, util.at(number[("scatter", q - 1, 2 * NT - 1)] + 1))
                for half in range(2):
                    ins = act.activation(Y[:, half * 512:half * 512 + 512], K.PS[:, 4 + half, :], ACT.Copy)
                ins.then_inc(copied.sem, copied.up())

            drains(0)
            for q in range(Q):
                act.wait_ge(released.sem, released.at(done("gate", q)))
                if q:
                    act.wait_ge(hidden.sem, hidden.at(q))
                for b in range(F // width):
                    ins = act.activation(GS[:, b * width:(b + 1) * width], K.PS[:, b, 0:width], ACT.Silu)
                ins.then_inc(silus.sem, silus.up())
                if q:
                    outputs(q - 1)
                if q + 1 < Q:
                    drains(q + 1)
                if turns > 1:
                    u = number[("turn", q, 1)]
                    act.wait_ge(util.sem, util.at(u + 1))
                    act.activation(HIDT[:, 512:1024], K.PS[:, 6 + u % 2, :], ACT.Copy
                                   ).then_inc(drained[u % 2].sem, drained[u % 2].up())
            outputs(Q - 1)


def experts(K, HT, tiles, E, F, C, logits, route, weights, label):
    NT = len(tiles)
    n_log = logits[1] - logits[0]
    rows = lambda a, n: K.AREA[:, a:a + n, :]
    H2 = rows(0, 8).rearrange("p (t a) n -> p t (a n)", a=2)
    ACC = rows(8, 8).rearrange("p (t a) n -> p t (a n)", a=2)
    own = K.counted("vector_step")
    filled, taken = K.counted("bank_filled"), K.counted("outputs_taken")
    with K.phase("token-major copy; router logits") as block:
        @block.tensor
        def _(pe):
            for i, t in enumerate(tiles):
                for half in range(2):
                    j = 2 * i + half
                    if j >= 4:
                        pe.wait_ge(taken.sem, taken.at(j - 3))
                    for k in range(4):
                        ins = pe.transpose(K.PS[:, 4 + j % 4, k * P:k * P + P],
                                           HT[:, 4 * half + k, t * P:t * P + P], K.IDENT[:, :])
                    ins.then_inc(filled.sem, filled.up())
            for i, t in enumerate(tiles):
                products(pe, K.PS[:, 0, i * n_log:(i + 1) * n_log],
                         [(HT[:, k, t * P:t * P + P], K.ROUT[:, k, logits[0]:logits[1]]) for k in range(KT)])

        @block.vector
        def _(v):
            for j in range(2 * NT):
                v.wait_ge(filled.sem, filled.at(j + 1))
                ins = v.tensor_copy(H2[:, j // 2, (j % 2) * 512:(j % 2) * 512 + 512], K.PS[:, 4 + j % 4, :])
                ins.then_inc(taken.sem, taken.up())
            v.memset(ACC, 0.0)

    route(K, NT)
    ranked = K.counted("scores_ready")
    with K.phase("places of the tokens in their experts") as block:
        @block.tensor
        def _(pe):
            for t in range(NT):
                pairs = [(K.ONES[:, :], K.RM[:, i, 0:E]) for i in range(t)] + [(K.STRICT[:, :], K.RM[:, t, 0:E])]
                ins = products(pe, K.PS[:, 1, t * E:(t + 1) * E], pairs)
            ins.then_inc(ranked.sem, ranked.up())

        @block.vector
        def _(v):
            for t in range(NT):
                ins = v.tensor_scalar(K.RP[:, t, 0:E], K.RM[:, t, 0:E], 1.0, -1e6, ALU.subtract, ALU.mult)
                ins.then_inc(own.sem, own.up())
                v.wait_ge(own.sem, own.last())
            v.wait_ge(ranked.sem, ranked.at(1))
            ins = v.tensor_tensor(K.RP[:, 0:NT, 0:E], K.RP[:, 0:NT, 0:E],
                                  K.PS[:, 1, 0:NT * E].rearrange("p (t e) -> p t e", t=NT), ALU.add)
            ins.then_inc(own.sem, own.up())
            v.wait_ge(own.sem, own.last())
            ins = v.tensor_scalar(K.RO[:, 0:NT, 0:E], K.RP[:, 0:NT, 0:E], float(C), None, ALU.is_ge)
            ins.then_inc(own.sem, own.up())
            v.wait_ge(own.sem, own.last())
            ins = v.tensor_tensor(K.RO[:, 0:NT, 0:E], K.RO[:, 0:NT, 0:E], K.RM[:, 0:NT, 0:E], ALU.mult)
            ins.then_inc(own.sem, own.up())
            v.wait_ge(own.sem, own.last())
            v.tensor_reduce(K.OVER[:, 0:1], K.RO[:, 0:NT, 0:E], AX.XY, ALU.add).then_inc(own.sem, own.up())
            v.wait_ge(own.sem, own.last())
            ins = v.tensor_tensor(K.RO[:, 0:NT, 0:E], K.RO[:, 0:NT, 0:E], K.RW[:, 0:NT, 0:E], ALU.mult)
            ins.then_inc(own.sem, own.up())
            v.wait_ge(own.sem, own.last())

    (paired_experts if C == P // 2 else single_experts)(K, NT, E, F, C, rows, H2, ACC)
    overflow(K, HT, tiles, E, F, weights, rows, label)

    streams = (0, 1) if NT == 4 else (0,)
    for s in streams:
        spread(K, lambda k, s=s: K.MOD[:, 40 + k, s:s + 1], K.GB[:, s, :])
    with K.phase("gated experts' sum") as block:
        @block.vector
        def _(v):
            for i, t in enumerate(tiles):
                s = 1 if t in CTX else 0
                v.tensor_tensor(ACC[:, i, :], ACC[:, i, :], K.GB[:, s, :], ALU.mult).then_inc(own.sem, own.up())
                v.wait_ge(own.sem, own.last())
                v.tensor_tensor(K.X[:, t, :], K.X[:, t, :], ACC[:, i, :], ALU.add)


def overflow(K, HT, tiles, E, F, weights, rows, label):
    NT, NC = len(tiles), F // CHUNK_COLS
    first, N = tiles[0] * P, len(tiles) * P
    gate_w, up_w, down_w = weights
    ACC = rows(8, 8).rearrange("p (t a) n -> p t (a n)", a=2)
    WG, WU, WD = (rows(a, 4).rearrange("p a n -> p (a n)").rearrange("p (k n) -> p k n", k=k)
                  for a, k in ((44, KT), (48, KT), (52, 2)))
    G, HID = rows(16, 2), rows(20, 2)
    new = lambda what: K.ctx.enter_context(K.nc.semaphore(f"left_{label}_{what}"))
    loaded, multiplied, activated, added = new("loaded"), new("multiplied"), new("activated"), new("added")
    counted, own = K.counted("scores_ready"), K.counted("vector_step")
    S = 1 + 2 * NT

    with K.phase("count of the tokens left over") as block:
        @block.tensor
        def _(pe):
            ins = pe.matmul(K.PS[:, 0, 0:1], K.ONES[:, :], K.OVER[:, 0:1], start=True, stop=True)
            ins.then_inc(counted.sem, counted.up())

        @block.vector
        def _(v):
            v.wait_ge(counted.sem, counted.at(1))
            v.tensor_copy(K.LEFT[:, :], K.PS[:, 0, 0:1]).then_inc(own.sem, own.up())
            v.wait_ge(own.sem, own.last())

    def any_left(eng):
        return eng.value_load(K.LEFT[0:1, 0:1], min_val=0, max_val=2 * NTOK)

    with K.phase("tokens left over") as block:
        @block.sync
        def _(sp):
            left = any_left(sp)
            with sp.If(left > 0):
                with sp.Fori(0, E) as e:
                    for c in range(NC):
                        sp.wait_ge(multiplied, e * (NC * S) + (c * S + 1))
                        cols = slice(c * CHUNK_COLS, (c + 1) * CHUNK_COLS)
                        sp.dma_start(WG, gate_w[bass.ds(e, 1), :, cols].rearrange("a (k p) n -> p (a k) n", p=P)
                                     ).then_inc(loaded, 16)
                        sp.dma_start(WU, up_w[bass.ds(e, 1), :, cols].rearrange("a (k p) n -> p (a k) n", p=P)
                                     ).then_inc(loaded, 16)
                        sp.dma_start(WD, down_w[bass.ds(e, 1), cols, :].rearrange("a (k p) n -> p (a k) n", p=P)
                                     ).then_inc(loaded, 16)

        @block.tensor
        def _(pe):
            left = any_left(pe)
            with pe.If(left > 0):
                pe.matmul(K.PS[:, 6, 0:1], K.ONES[:, :], K.ONES[:, 0:1], start=True, stop=True
                          ).then_inc(multiplied, 1)
                with pe.Fori(0, E) as e:
                    for c in range(NC):
                        pe.wait_ge(loaded, e * (NC * 48) + (c + 1) * 48)
                        pe.wait_ge(added, e * (NC * S) + (c * S + 1))
                        for m, w in enumerate((WG, WU)):
                            for f in range(2):
                                ins = products(pe, K.PS[:, 2 * m + f, 0:N],
                                               [(w[:, k, f * P:f * P + P], HT[:, k, first:first + N])
                                                for k in range(KT)])
                        ins.then_inc(multiplied, 1)
                        pe.wait_ge(added, e * (NC * S) + (c * S + 2))
                        for j in range(2 * NT):
                            if j >= 2:
                                pe.wait_ge(added, e * (NC * S) + (c * S + 1 + j))
                            products(pe, K.PS[:, 4 + j % 2, :],
                                     [(HID[:, k, (j // 2) * P:(j // 2) * P + P],
                                       WD[:, k, (j % 2) * 512:(j % 2) * 512 + 512]) for k in range(2)]
                                     ).then_inc(multiplied, 1)

        @block.scalar
        def _(act):
            left = any_left(act)
            with act.If(left > 0):
                with act.Fori(0, E) as e:
                    for c in range(NC):
                        act.wait_ge(multiplied, e * (NC * S) + (c * S + 2))
                        act.activation(G[:, :, 0:N], K.PS[:, 0:2, 0:N], ACT.Silu).then_inc(activated, 1)

        @block.vector
        def _(v):
            left = any_left(v)
            with v.If(left > 0):
                v.memset(K.OVER[:, 1:2], 0.0).then_inc(added, 1)
                with v.Fori(0, E) as e:
                    for c in range(NC):
                        v.wait_ge(activated, e * NC + (c + 1))
                        if c == 0:
                            v.tensor_copy(K.LW[:, 0:NT], K.RO[:, 0:NT, bass.ds(e, 1)].rearrange("p t o -> p (t o)"))
                        v.tensor_tensor(HID[:, :, 0:N], G[:, :, 0:N], K.PS[:, 2:4, 0:N], ALU.mult).then_inc(added, 1)
                        v.wait_ge(added, e * (NC * S) + (c * S + 2))
                        for j in range(2 * NT):
                            v.wait_ge(multiplied, e * (NC * S) + (c * S + 3 + j))
                            a = ACC[:, j // 2, (j % 2) * 512:(j % 2) * 512 + 512]
                            v.scalar_tensor_tensor(a, K.PS[:, 4 + j % 2, :], K.LW[:, j // 2:j // 2 + 1], a,
                                                   ALU.mult, ALU.add).then_inc(added, 1)


def shape_constants():
    i = np.arange(P)
    masks = [np.eye(P, dtype=bool)]
    for level in LEVELS:
        same = (i[:, None] // (2 * level)) == (i[None, :] // (2 * level))
        left = (i % (2 * level)) < level
        masks.append(same & left[:, None] & ~left[None, :])
        masks.append(same & ~left[:, None] & left[None, :])
    pos = np.arange(256)
    inv = (1.0 / (np.float32(10000.0) ** (np.arange(0, 32, 2, dtype=np.float32) / np.float32(32)))).astype(np.float32)
    ar = (pos // 64).astype(np.float32)[:, None] * inv
    ac = (pos % 64).astype(np.float32)[:, None] * inv
    ang = np.concatenate([ar, ar, ac, ac], axis=-1).astype(np.float64)
    sign = np.concatenate([-np.ones(16), np.ones(16)] * 2)
    rope = np.concatenate([np.cos(ang), np.sin(ang) * sign], axis=1).astype(np.float32)
    band = np.where(np.abs(pos[:, None] - pos[None, :]) <= 128, 0.0, NEG).astype(np.float32)
    band = np.concatenate([np.zeros((256, 256), np.float32), band], axis=1)
    causal = np.concatenate([np.zeros((P, P)), np.where(i[None, :] <= i[:, None], 0.0, NEG)], axis=1)
    before = [np.broadcast_to((np.arange(n)[None, :] < np.arange(n)[:, None]).reshape(-1), (P, n * n)) for n in (4, 8)]
    return {
        "c_ident": np.eye(P, dtype=np.float32),
        "c_masks": np.stack(masks, axis=1).astype(np.float32),
        "c_rope": rope,
        "c_band": band,
        "c_causal": causal.astype(np.float32),
        "c_strict": (i[:, None] < i[None, :]).astype(np.float32),
        "c_before": np.concatenate(before, axis=1).astype(np.float32),
        "c_iota": np.arange(P, dtype=np.float32),
        "c_inv": (1.0 / (np.float32(10000.0) ** (np.arange(0, 64, 2, dtype=np.float32) / np.float32(64)))).astype(np.float32),
    }


def build(nc, A, C, out, stop=None):
    with ExitStack() as ctx:
        K = Core(nc, ctx)
        K.PS = ctx.enter_context(nc.psum_tensor("PS", [P, 8, 512], F32))
        K.ring = K.sb("ring", [P, RING * SLOT])
        K.X = K.sb("X", [P, 4, D])
        K.SQ = K.sb("SQ", [P, D])
        K.AREA = K.sb("AREA", [P, 58, 512])
        take = lambda a, n: K.AREA[:, a:a + n, :]
        K.BIG, K.FM, K.LF, K.VB, K.GA = take(0, 8), take(8, 8), take(16, 8), take(24, 4), take(28, 4)
        K.YN = K.BIG.rearrange("p (t a) n -> p t (a n)", a=2)
        HT, YT = take(32, 8), take(44, 8)
        K.EX = take(16, 4).rearrange("p (s m) n -> p s m n", s=2)
        K.LG, K.AW, K.AWT = take(20, 2), take(22, 2), take(28, 2)
        K.HW, K.HA, K.HQ = take(32, 6), take(38, 2), take(40, 4)
        K.ST = take(52, 6).rearrange("p (d i) n -> p d i n", d=2)
        K.OUTB = take(12, 4)
        K.GB = take(16, 4).rearrange("p (s a) n -> p s (a n)", s=2)
        K.IDENT, K.ONES, K.STRICT = (K.sb(n, [P, P]) for n in ("IDENT", "ONES", "STRICT"))
        K.MASKS = K.sb("MASKS", [P, 1 + 2 * len(LEVELS), P], U8)
        K.MASKS32 = take(2, 4).rearrange("p a n -> p (a n)")[:, 0:(1 + 2 * len(LEVELS)) * P].rearrange(
            "p (m n) -> p m n", n=P)
        K.ROPE = K.sb("ROPE", [P, 2, 128])
        K.BAND = K.sb("BAND", [P, 2, 512])
        K.CAUSAL = K.sb("CAUSAL", [P, 256])
        K.BEFORE = K.sb("BEFORE", [P, 80])
        K.IOTA = K.sb("IOTA", [P, P])
        K.INV = K.sb("INV", [P, 32])
        K.VROW = take(0, 1).rearrange("p a (t n) -> p (a t) n", n=P)
        K.COL = K.sb("COL", [P, 384])
        K.DLAM, K.DL = K.AREA[:, 1, 0:256], K.sb("DL", [P, 256])
        K.LB = K.sb("LB", [P, 4, 8])
        K.CS = K.sb("CS", [P, KT, 4])
        K.MOD = K.sb("MOD", [P, 48, 2])
        K.AFF = K.sb("AFF", [P, 2, KT, 2])
        K.SINK = K.sb("SINK", [P, 16])
        K.SUBLN = K.sb("SUBLN", [P, 1])
        K.QKN = K.sb("QKN", [P, 2, 192])
        K.ROUT = K.sb("ROUT", [P, KT, 52])
        K.RB = K.sb("RB", [P, 52])
        K.RW, K.RM, K.RP, K.RO = (K.sb(n, [P, 4, 32]) for n in ("RW", "RM", "RP", "RO"))
        K.RT, K.OVER = K.sb("RT", [P, 96]), K.sb("OVER", [P, 2])
        K.LEFT, K.LW = K.sb("LEFT", [P, 1], I32), K.sb("LW", [P, 4])
        K.STAT = K.sb("STAT", [P, 16])
        K.MX = K.sb("MX", [P, 2, 8])
        K.TOT = K.sb("TOT", [P, 2, 4])
        K.POSI, K.POSR = K.sb("POSI", [P, 2], I32), K.sb("POSR", [P, 256], I32)
        K.POSF, K.SPL = K.sb("POSF", [P, 2]), K.sb("SPL", [P, 12])
        K.POSG = K.AREA[:, 53, :].rearrange("p (a n) -> p a n", a=2)
        K.ANG, K.TURNS = (K.AREA[:, 52, a:a + P].rearrange("p (t s n) -> p t s n", t=2, s=2) for a in (0, P))
        K.TRIG = K.AREA[:, 52, 2 * P:4 * P].rearrange("p (t s n) -> p t s n", t=2, s=2)

        tiled = lambda a: a.rearrange("(k p) -> k p", p=P)
        flat = lambda a: a.rearrange("a (k p) -> (a k) p", p=P)
        K.vectors = [
            ("c", flat(A["c"])), ("c_ctx", tiled(A["c_ctx"])), ("c_2", flat(A["c_2"])),
            ("ada_b0", tiled(A["ada_b"][0])), ("ada_b1", tiled(A["ada_b"][1])), ("ada_b2", flat(A["b_ada_2"])),
            ("mix0", tiled(A["norm_mix_g"][0])), ("mix1", tiled(A["norm_mix_g"][1])),
            ("ffn0", tiled(A["norm_ffn_g"][0])), ("ffn1", tiled(A["norm_ffn_g"][1])),
            ("norm1", flat(A["norm1_g_2"])), ("norm2", flat(A["norm2_g_2"])), ("final", tiled(A["final_norm_g"])),
            ("lb", A["hgrn_lb_logits"].rearrange("l d (k p) -> (l d k) p", p=P)),
            ("hgrn_onorm", A["hgrn_onorm_g"]), ("subln", A["diff_subln_g"]),
            ("q_a", flat(A["q_a_norm_2"])), ("kv_a", flat(A["kv_a_norm_2"])),
            ("conv_w", A["conv_w_2"].rearrange("a i (k p) -> (a i k) p", p=P)), ("conv_b", flat(A["conv_b_2"])),
            ("lru_ba", flat(A["lru_ba_2"])), ("lru_bx", flat(A["lru_bx_2"])), ("lambda", flat(A["lru_lambda_2"])),
            ("lru_out", flat(A["lru_out_norm_2"])), ("attn_out", flat(A["attn_out_norm_2"])),
        ]

        def expert_chunk(gate, up, down, matrix, e, c):
            w = {"gate": gate, "up": up, "down": down}[matrix][e]
            return columns(w, c) if w.shape[0] == D else w.rearrange("(k p) n -> p k n", p=P)

        G = lambda name, layer: A[name][layer]
        K.chunks = [columns(A["ada_w"][0], c) for c in range(24)]
        K.chunks += [columns(A["even_w_in"][0], c) for c in (*range(10, 16), *range(10))]
        K.chunks += [columns(A["even_w_out"][0], c) for c in range(4)]
        first_moe = ("moe_w_gate", "moe_w_up", "moe_w_down")
        second_moe = ("w_gate_2", "w_up_2", "w_down_2")
        K.chunks += [expert_chunk(*(G(n, 0) for n in first_moe), m, e, c)
                     for e in range(16) for m in ("gate", "up", "down") for c in range(4)]
        K.chunks += [columns(A["ada_w"][1], c) for c in range(24)]
        K.chunks += [columns(A["odd_w_qkv"][0], c) for c in range(6)]
        K.chunks += [columns(A["odd_w_out"][0], c) for c in range(4)]
        K.chunks += [expert_chunk(*(G(n, 1) for n in first_moe), *at) for at in pair_order(16, D)]
        K.chunks += [columns(A["w_ada_2"][0], c) for c in range(24)]
        K.chunks += [columns(A["w_in_2"][0], 0), A["w_in_2"][0][:, 256:448].rearrange("(k p) n -> p k n", p=P)]
        K.chunks += [A["w_in_2"][0][:, 448 + 256 * c:704 + 256 * c].rearrange("(k p) n -> p k n", p=P) for c in range(4)]
        K.chunks += [A["w_q_b_2"][0].rearrange("(k p) n -> p k n", p=P),
                     A["w_kv_b_2"][0].rearrange("(k p) n -> p k n", p=P),
                     A["lru_wa_2"][0].rearrange("h i j -> i h j"), A["lru_wx_2"][0].rearrange("h i j -> i h j")]
        K.chunks += [columns(A["w_out_2"][0], c) for c in range(4)]
        K.chunks += [expert_chunk(*(G(n, 0) for n in second_moe), *at) for at in pair_order(32, 256)]

        def stages():
            load_constants(K, A, C)
            yield "constants"
            all_tiles = CTX + LAT
            modulation(K, "ada_b0", (0, 1), "mix0", "ffn0")
            modulated(K, 0, all_tiles, HT)
            yield "h0"
            diff_attention(K, A, HT, YT)
            yield "diff"
            hgrn2(K, A, HT, YT)
            yield "hgrn"
            gated_residual(K, all_tiles, YT, 2)
            modulated(K, 1, all_tiles, HT)
            yield "mix0"
            experts(K, HT, all_tiles, 16, 1024, CAP[0], (0, 16), route_first, [G(n, 0) for n in first_moe], 0)
            yield "moe0"
            modulation(K, "ada_b1", (0, 1), "mix1", "ffn1")
            modulated(K, 0, all_tiles, HT)
            window_attention(K, A, HT, YT)
            yield "swa"
            gated_residual(K, LAT, YT, 2)
            modulated(K, 1, LAT, HT)
            yield "mix1"
            experts(K, HT, LAT, 16, 1024, CAP[1], (0, 16), route_first, [G(n, 1) for n in first_moe], 1)
            normalise(K, LAT, D, lambda t: K.X[:, t:t + 1, :], lambda t: K.YN[:, t:t + 1, :])
            spread(K, lambda k: K.col("final", 1, k), K.GB[:, 0, :])
            with K.phase("final norm's gain") as block:
                @block.vector
                def _(v):
                    for t in LAT:
                        v.tensor_tensor(K.X[:, t, :], K.YN[:, t, :], K.GB[:, 0, :], ALU.mult)
            yield "first"
            modulation(K, "ada_b2", (2,), "norm1", "norm2")
            modulated(K, 0, LAT, HT)
            latent_attention(K, A, HT, YT)
            yield "mla"
            lru(K, A, YT)
            yield "lru"
            gated_residual(K, LAT, YT, 2)
            modulated(K, 1, LAT, HT)
            yield "mix2"
            experts(K, HT, LAT, 32, 256, CAP[2], (16, 52), route_second, [G(n, 0) for n in second_moe], 2)
            yield "end"

        for name in stages():
            if name == stop:
                break
        stored = ctx.enter_context(nc.semaphore("output_stored"))
        with K.phase("store") as block:
            @block.sync
            def _(sp):
                sp.dma_start(out[0].rearrange("(t p) d -> p t d", p=P), K.X[:, 2:4, :]).then_inc(stored, 16)
                sp.wait_ge(stored, 16)
                for i in range(RING):
                    n = len([m for m in range(K.issued) if m % RING == i])
                    if n:
                        sp.wait_ge(K.landed[i], 16 * n)


def kernel(**inputs):
    import concourse.bacc as bacc
    from concourse.bass_utils import run_bass_kernel_spmd

    nc = bacc.Bacc("TRN2", target_bir_lowering=False, num_devices=1)
    arrays, A, C = {}, {}, {}
    for group, items in ((A, inputs), (C, shape_constants())):
        for name, a in items.items():
            a = np.ascontiguousarray(a)
            arrays[name + "_in"] = a
            group[name] = nc.dram_tensor(name + "_in", a.shape, mybir.dt.from_np(a.dtype), kind="ExternalInput").ap()
    out = nc.dram_tensor("out", (1, 256, D), F32, kind="ExternalOutput").ap()
    build(nc, A, C, out)
    result = run_bass_kernel_spmd(nc, [arrays], core_ids=[0])
    return result.results[0]["out"]
```
